# Optimizing a Trainium2 kernel written in Bass

```python
import math
import jax, jax.numpy as jnp
from jax import lax
import numpy as np
import jax
import jax.numpy as jnp

D_MODEL = 1024
BATCH = 1
SEQ = 512
DEPTH = 2

GRID_W = 64
CTX_LEN = 256
N_MIXERS = 2
NORM_EPS = 1e-6

DN_QK_HEADS = 8
DN_V_HEADS = 16
DN_HEAD_K = 128
DN_HEAD_V = 128
DN_KEY_DIM = DN_QK_HEADS * DN_HEAD_K
DN_VAL_DIM = DN_V_HEADS * DN_HEAD_V
DN_CONV_DIM = 2 * DN_KEY_DIM + DN_VAL_DIM
DN_CONV_K = 5
DN_CHUNK = 64
DN_IN_DIM = DN_CONV_DIM + DN_VAL_DIM + 4 * DN_V_HEADS
DT_MIN = 0.001
DT_MAX = 0.1

ATT_Q_HEADS = 8
ATT_KV_HEADS = 2
ATT_HEAD_DIM = 128
ATT_Q_DIM = ATT_Q_HEADS * ATT_HEAD_DIM
ATT_KV_DIM = ATT_KV_HEADS * ATT_HEAD_DIM
ATT_IN_DIM = ATT_Q_DIM + 2 * ATT_KV_DIM + ATT_Q_DIM
ATT_BLOCK = 128
ROPE_THETA = 10000.0

N_DN_LAYERS = (DEPTH + N_MIXERS - 1) // N_MIXERS
N_ATT_LAYERS = DEPTH // N_MIXERS


F32 = jnp.float32

def rms_norm(x, g):
    xf = x.astype(F32)
    y = xf * lax.rsqrt(jnp.mean(xf * xf, axis=-1, keepdims=True) + NORM_EPS)
    return (y * g.astype(F32)).astype(x.dtype)

def l2_norm(x):
    xf = x.astype(F32)
    return (xf * lax.rsqrt(jnp.sum(xf * xf, axis=-1, keepdims=True) + NORM_EPS)).astype(x.dtype)

def centred_dwconv(x, w):
    k = w.shape[0]
    return lax.conv_general_dilated(x, w[:, None, :].astype(x.dtype), window_strides=(1,),
                                    padding=[(k // 2, k // 2)],
                                    dimension_numbers=('NWC', 'WIO', 'NWC'),
                                    feature_group_count=x.shape[-1])

def chunk_gated_delta(q, k, v, g, beta, s0):
    b, h, l, dk = k.shape
    dv = v.shape[-1]
    n = l // DN_CHUNK
    q = q.astype(F32) * (dk ** -0.5)
    k = k.astype(F32)
    v32 = v.astype(F32)
    ch = lambda t: t.reshape(b, h, n, DN_CHUNK, *t.shape[3:])
    qc, kc, vc = ch(q), ch(k), ch(v32)
    gc = jnp.cumsum(ch(g.astype(F32)), axis=-1)
    bc = ch(beta.astype(F32))
    idx = jnp.arange(DN_CHUNK)
    lower = idx[:, None] >= idx[None, :]
    strict = idx[:, None] > idx[None, :]
    decay = jnp.exp(jnp.where(lower, gc[..., :, None] - gc[..., None, :], -jnp.inf))
    kb = kc * bc[..., None]
    vb = vc * bc[..., None]
    a = jnp.where(strict, jnp.einsum('bhncd,bhnsd->bhncs', kb, kc) * decay, 0.0)
    eye = jnp.eye(DN_CHUNK, dtype=F32)
    t_inv = lax.linalg.triangular_solve(eye + a, jnp.broadcast_to(eye, a.shape),
                                        left_side=True, lower=True, unit_diagonal=True)
    u = jnp.einsum('bhncs,bhnse->bhnce', t_inv, vb)
    w = jnp.einsum('bhncs,bhnsd->bhncd', t_inv, kb * jnp.exp(gc)[..., None])
    qk = jnp.einsum('bhncd,bhnsd->bhncs', qc, kc) * decay
    q_dec = qc * jnp.exp(gc)[..., None]
    k_dec = kc * jnp.exp(gc[..., -1:] - gc)[..., None]
    g_last = jnp.exp(gc[..., -1])

    def step(s, xs):
        qk_i, qd_i, kd_i, u_i, w_i, gl_i = xs
        v_new = u_i - jnp.einsum('bhcd,bhde->bhce', w_i, s)
        o = jnp.einsum('bhcd,bhde->bhce', qd_i, s) + jnp.einsum('bhcs,bhse->bhce', qk_i, v_new)
        s = s * gl_i[..., None, None] + jnp.einsum('bhcd,bhce->bhde', kd_i, v_new)
        return s, o

    xs = tuple(jnp.moveaxis(t_, 2, 0) for t_ in (qk, q_dec, k_dec, u, w, g_last))
    s_fin, o = lax.scan(step, s0.astype(F32), xs)
    o = jnp.moveaxis(o, 0, 2).reshape(b, h, l, dv)
    return o.astype(v.dtype), s_fin

def bidir_delta(q, k, v, g, beta, s0_f, s0_b):
    o_f, s_f = chunk_gated_delta(q, k, v, g[:, 0], beta[:, 0], s0_f)
    fl = lambda t: jnp.flip(t, axis=2)
    o_b, s_b = chunk_gated_delta(fl(q), fl(k), fl(v), fl(g[:, 1]), fl(beta[:, 1]), s0_b)
    return o_f + fl(o_b), s_f, s_b

def deltanet_mixer(u_lat, u_ctx, w_in, conv_w, a_log, dt_bias, o_norm_g, w_out, need_ctx):
    def branch_inputs(u):
        b, l, _ = u.shape
        p = u @ w_in
        qkv = jax.nn.silu(centred_dwconv(p[..., :DN_CONV_DIM], conv_w))
        z = p[..., DN_CONV_DIM:DN_CONV_DIM + DN_VAL_DIM]
        ab = p[..., DN_CONV_DIM + DN_VAL_DIM:].reshape(b, l, 2, 2, DN_V_HEADS).astype(F32)
        q, k, v = jnp.split(qkv, [DN_KEY_DIM, 2 * DN_KEY_DIM], axis=-1)
        rep = DN_V_HEADS // DN_QK_HEADS
        q = jnp.repeat(l2_norm(q.reshape(b, l, DN_QK_HEADS, DN_HEAD_K)), rep, axis=2)
        k = jnp.repeat(l2_norm(k.reshape(b, l, DN_QK_HEADS, DN_HEAD_K)), rep, axis=2)
        v = v.reshape(b, l, DN_V_HEADS, DN_HEAD_V)
        beta = jax.nn.sigmoid(ab[:, :, 0])
        g = -jnp.exp(a_log.astype(F32)) * jax.nn.softplus(ab[:, :, 1] + dt_bias.astype(F32))
        bhl = lambda t: jnp.transpose(t, (0, 2, 1, 3))
        return bhl(q), bhl(k), bhl(v), jnp.transpose(g, (0, 2, 3, 1)), jnp.transpose(beta, (0, 2, 3, 1)), z

    def finish(o, z):
        b, h, l, dv = o.shape
        o = rms_norm(jnp.transpose(o, (0, 2, 1, 3)), o_norm_g).astype(z.dtype)
        return (o.reshape(b, l, DN_VAL_DIM) * jax.nn.silu(z)) @ w_out

    qc, kc, vc, gc, bc, zc = branch_inputs(u_ctx)
    s_zero = jnp.zeros((u_ctx.shape[0], DN_V_HEADS, DN_HEAD_K, DN_HEAD_V), F32)
    o_ctx, s_f, s_b = bidir_delta(qc, kc, vc, gc, bc, s_zero, s_zero)
    ql, kl, vl, gl, bl, zl = branch_inputs(u_lat)
    o_lat, _, _ = bidir_delta(ql, kl, vl, gl, bl, s_f, s_b)
    y_lat = finish(o_lat, zl)
    y_ctx = finish(o_ctx, zc) if need_ctx else None
    return y_lat, y_ctx

def axial_rope_angles(n):
    rows = n // GRID_W
    row = jnp.broadcast_to(jnp.arange(rows)[:, None], (rows, GRID_W)).reshape(-1).astype(F32)
    col = jnp.broadcast_to(jnp.arange(GRID_W)[None, :], (rows, GRID_W)).reshape(-1).astype(F32)
    axis_dim = ATT_HEAD_DIM // 2
    inv = ROPE_THETA ** (-jnp.arange(0, axis_dim, 2, dtype=F32) / axis_dim)
    return row[:, None] * inv, col[:, None] * inv

def rope_rotate(x, ang):
    x1, x2 = jnp.split(x, 2, axis=-1)
    cos = jnp.cos(ang)[:, None, :].astype(x.dtype)
    sin = jnp.sin(ang)[:, None, :].astype(x.dtype)
    return jnp.concatenate([x1 * cos - x2 * sin, x2 * cos + x1 * sin], axis=-1)

def apply_axial_rope(x, ang_r, ang_c):
    xr, xc = jnp.split(x, 2, axis=-1)
    return jnp.concatenate([rope_rotate(xr, ang_r), rope_rotate(xc, ang_c)], axis=-1)

def gqa_attend(q, k, v):
    b, lq, hq, d = q.shape
    qg = q.reshape(b, lq, ATT_KV_HEADS, hq // ATT_KV_HEADS, d)
    s = jnp.einsum('bqhgd,bkhd->bhgqk', qg, k).astype(F32) * (d ** -0.5)
    p = jax.nn.softmax(s, axis=-1).astype(v.dtype)
    return jnp.einsum('bhgqk,bkhd->bqhgd', p, v).reshape(b, lq, hq, d)

def blocked_gqa(q, k, v):
    b, lq, hq, d = q.shape
    nb = lq // ATT_BLOCK
    qb = jnp.moveaxis(q.reshape(b, nb, ATT_BLOCK, hq, d), 1, 0)
    ob = lax.map(lambda qi: gqa_attend(qi, k, v), qb)
    return jnp.moveaxis(ob, 0, 1).reshape(b, lq, hq, d)

def attention_mixer(u_lat, u_ctx, w_in, q_norm_g, k_norm_g, w_out, need_ctx):
    def project(u):
        b, l, _ = u.shape
        p = u @ w_in
        q, k, v, z = jnp.split(p, [ATT_Q_DIM, ATT_Q_DIM + ATT_KV_DIM, ATT_Q_DIM + 2 * ATT_KV_DIM], axis=-1)
        q = rms_norm(q.reshape(b, l, ATT_Q_HEADS, ATT_HEAD_DIM), q_norm_g)
        k = rms_norm(k.reshape(b, l, ATT_KV_HEADS, ATT_HEAD_DIM), k_norm_g)
        v = v.reshape(b, l, ATT_KV_HEADS, ATT_HEAD_DIM)
        return q, k, v, z

    def finish(o, z):
        b, l = o.shape[:2]
        return (o.reshape(b, l, ATT_Q_DIM) * jax.nn.silu(z)) @ w_out

    qc, kc, vc, zc = project(u_ctx)
    ql, kl, vl, zl = project(u_lat)
    ang_r, ang_c = axial_rope_angles(u_lat.shape[1])
    ql = apply_axial_rope(ql, ang_r, ang_c)
    kl = apply_axial_rope(kl, ang_r, ang_c)
    k_all = jnp.concatenate([kc, kl], axis=1)
    v_all = jnp.concatenate([vc, vl], axis=1)
    y_lat = finish(blocked_gqa(ql, k_all, v_all), zl)
    y_ctx = finish(gqa_attend(qc, kc, vc), zc) if need_ctx else None
    return y_lat, y_ctx

def first_inputs(seed: int = 0) -> dict:
    key = jax.random.key(seed)
    ks = jax.random.split(key, 20)
    nrm = lambda k, shape, scale: jax.random.normal(k, shape, F32) * scale
    d = D_MODEL
    n_dn, n_att = N_DN_LAYERS, N_ATT_LAYERS
    a_log = jnp.log(jax.random.uniform(ks[8], (n_dn, 2, DN_V_HEADS), F32, 1.0, 16.0))
    dt = jnp.exp(jax.random.uniform(ks[9], (n_dn, 2, DN_V_HEADS), F32, math.log(DT_MIN), math.log(DT_MAX)))
    dt_bias = dt + jnp.log(-jnp.expm1(-dt))
    return {
        'x': nrm(ks[0], (BATCH, SEQ, d), 1.0),
        'c': nrm(ks[1], (BATCH, d), 1.0),
        'ctx': nrm(ks[2], (BATCH, CTX_LEN, d), 1.0),
        'c_ctx': nrm(ks[3], (d,), 1.0),
        'norm_g': 1.0 + nrm(ks[4], (DEPTH, d), 0.02),
        'ada_w': nrm(ks[5], (DEPTH, d, 3 * d), 0.5 * d ** -0.5),
        'ada_b': nrm(ks[6], (DEPTH, 3 * d), 0.02),
        'dn_w_in': nrm(ks[7], (n_dn, d, DN_IN_DIM), d ** -0.5),
        'dn_conv_w': nrm(ks[10], (n_dn, DN_CONV_K, DN_CONV_DIM), DN_CONV_K ** -0.5),
        'dn_a_log': a_log,
        'dn_dt_bias': dt_bias,
        'dn_o_norm_g': 1.0 + nrm(ks[11], (n_dn, DN_HEAD_V), 0.02),
        'dn_w_out': nrm(ks[12], (n_dn, DN_VAL_DIM, d), DN_VAL_DIM ** -0.5),
        'att_w_in': nrm(ks[13], (n_att, d, ATT_IN_DIM), d ** -0.5),
        'att_q_norm_g': 1.0 + nrm(ks[14], (n_att, ATT_HEAD_DIM), 0.02),
        'att_k_norm_g': 1.0 + nrm(ks[15], (n_att, ATT_HEAD_DIM), 0.02),
        'att_w_out': nrm(ks[16], (n_att, ATT_Q_DIM, d), ATT_Q_DIM ** -0.5),
        'final_norm_g': 1.0 + nrm(ks[17], (d,), 0.02),
    }

def first_block(x, c, ctx, c_ctx, norm_g, ada_w, ada_b, dn_w_in, dn_conv_w, dn_a_log, dn_dt_bias,
              dn_o_norm_g, dn_w_out, att_w_in, att_q_norm_g, att_k_norm_g, att_w_out, final_norm_g):
    h_lat, h_ctx = x, ctx
    sc_lat, sc_ctx = jax.nn.silu(c), jax.nn.silu(c_ctx)
    for i in range(DEPTH):
        need_ctx = i < DEPTH - 1
        shift, scale, gate = jnp.split(sc_lat @ ada_w[i] + ada_b[i], 3, axis=-1)
        shift_c, scale_c, gate_c = jnp.split(sc_ctx @ ada_w[i] + ada_b[i], 3, axis=-1)
        u_lat = rms_norm(h_lat, norm_g[i]) * (1.0 + scale[:, None]) + shift[:, None]
        u_ctx = rms_norm(h_ctx, norm_g[i]) * (1.0 + scale_c) + shift_c
        j = i // N_MIXERS
        if i % N_MIXERS == 0:
            y_lat, y_ctx = deltanet_mixer(u_lat, u_ctx, dn_w_in[j], dn_conv_w[j], dn_a_log[j], dn_dt_bias[j],
                                          dn_o_norm_g[j], dn_w_out[j], need_ctx)
        else:
            y_lat, y_ctx = attention_mixer(u_lat, u_ctx, att_w_in[j], att_q_norm_g[j], att_k_norm_g[j],
                                           att_w_out[j], need_ctx)
        h_lat = h_lat + gate[:, None] * y_lat
        if need_ctx:
            h_ctx = h_ctx + gate_c * y_ctx
    return rms_norm(h_lat, final_norm_g)


EPS = 1e-6

MLSTM_HEADS = 8
MLSTM_DQK = 64
MLSTM_DV = 64
MLSTM_CONV = 3
MLSTM_CHUNK = 64
DIFF_HEADS = 4
DIFF_DQK = 64
DIFF_DV = 128
ROPE_BASE = 10000.0
Q_BLOCK = 128
CONV_WIDTH = 31
D_FF = 2816
N_EXPERTS = 8
TOP_K = 2
D_FF_EXPERT = 2816
MOE_BLOCK = 128

MQK = MLSTM_HEADS * MLSTM_DQK
MV = MLSTM_HEADS * MLSTM_DV
MG = 4 * MLSTM_HEADS
DQK = DIFF_HEADS * 2 * DIFF_DQK
DVW = DIFF_HEADS * DIFF_DV
OFF_MQ = 0
OFF_MK = OFF_MQ + MQK
OFF_MV = OFF_MK + MQK
OFF_MO = OFF_MV + MV
OFF_MG = OFF_MO + MV
OFF_DQ = OFF_MG + MG
OFF_DK = OFF_DQ + DQK
OFF_DV = OFF_DK + DQK
IN0_WIDTH = OFF_DV + DVW
MIX0_WIDTH = MV + DVW


F32_2 = jnp.float32

def rmsnorm(x, g):
    xf = x.astype(F32_2)
    y = xf * lax.rsqrt(jnp.mean(xf * xf, axis=-1, keepdims=True) + EPS)
    return (y * g.astype(F32_2)).astype(x.dtype)

def layernorm(x, g, b):
    xf = x.astype(F32_2)
    mu = jnp.mean(xf, axis=-1, keepdims=True)
    var = jnp.mean(jnp.square(xf - mu), axis=-1, keepdims=True)
    return ((xf - mu) * lax.rsqrt(var + EPS) * g.astype(F32_2) + b.astype(F32_2)).astype(x.dtype)

def adaln(cond, w, b):
    return jax.nn.silu(cond) @ w + b

def modulate(x, g, shift, scale):
    return rmsnorm(x, g) * (1 + scale) + shift

def depthwise_conv(x, w):
    k = w.shape[0]
    return lax.conv_general_dilated(
        x, w[:, None, :].astype(x.dtype), window_strides=(1,),
        padding=[((k - 1) // 2, k // 2)], dimension_numbers=('NWC', 'WIO', 'NWC'),
        feature_group_count=x.shape[-1])

def to_heads(a, n_heads):
    b, t, _ = a.shape
    return a.reshape(b, t, n_heads, -1).transpose(0, 2, 1, 3)

def axial_rope_tables(t_len):
    rows = t_len // GRID_W
    row = jnp.repeat(jnp.arange(rows, dtype=F32_2), GRID_W)
    col = jnp.tile(jnp.arange(GRID_W, dtype=F32_2), rows)
    axis_dim = DIFF_DQK // 2
    inv = ROPE_BASE ** (-jnp.arange(0, axis_dim, 2, dtype=F32_2) / axis_dim)
    ang_r = row[:, None] * inv
    ang_c = col[:, None] * inv
    return jnp.cos(ang_r), jnp.sin(ang_r), jnp.cos(ang_c), jnp.sin(ang_c)

def rotate(x, cos, sin):
    x1, x2 = jnp.split(x, 2, axis=-1)
    return jnp.concatenate([x1 * cos - x2 * sin, x2 * cos + x1 * sin], axis=-1)

def apply_axial_rope_2(x, tables):
    cr, sr, cc, sc = tables
    xr, xc = jnp.split(x.astype(F32_2), 2, axis=-1)
    return jnp.concatenate([rotate(xr, cr, sr), rotate(xc, cc, sc)], axis=-1).astype(x.dtype)

def mlstm_gates(g, gate_b):
    g = (g + gate_b).astype(F32_2)
    b, t, _ = g.shape
    g = g.reshape(b, t, 4, MLSTM_HEADS).transpose(2, 0, 3, 1)
    return g[0], jax.nn.log_sigmoid(g[1]), g[2], jax.nn.log_sigmoid(g[3])

def mlstm_state_update(C, n, m, k, v, ig, b):
    b_last = b[..., -1]
    log_s = b_last[..., None] - b + ig
    m_new = jnp.maximum(b_last + m, jnp.max(log_s, axis=-1))
    ws = jnp.exp(log_s - m_new[..., None])
    decay = jnp.exp(b_last + m - m_new)
    C_new = decay[..., None, None] * C + jnp.einsum('bhs,bhsd,bhse->bhde', ws, k, v)
    n_new = decay[..., None] * n + jnp.einsum('bhs,bhsd->bhd', ws, k)
    return C_new, n_new, m_new

def mlstm_chunk(carry, inp):
    C, n, m = carry
    q, k, v, ig, lf = inp
    L = q.shape[2]
    b = jnp.cumsum(lf, axis=-1)
    order = jnp.tril(jnp.ones((L, L), dtype=bool))
    log_d = jnp.where(order, b[..., :, None] - b[..., None, :] + ig[..., None, :], -jnp.inf)
    log_inter = b + m[..., None]
    m_t = jnp.maximum(log_inter, jnp.max(log_d, axis=-1))
    s = jnp.einsum('bhtd,bhsd->bhts', q, k) * jnp.exp(log_d - m_t[..., None])
    w_inter = jnp.exp(log_inter - m_t)
    num = w_inter[..., None] * jnp.einsum('bhtd,bhde->bhte', q, C) + jnp.einsum('bhts,bhse->bhte', s, v)
    den = w_inter * jnp.einsum('bhtd,bhd->bht', q, n) + jnp.sum(s, axis=-1)
    h = num / jnp.maximum(jnp.abs(den), jnp.exp(-m_t))[..., None]
    return mlstm_state_update(C, n, m, k, v, ig, b), h

def mlstm_scan(q, k, v, ig, lf, state):
    b, h, t, _ = q.shape
    nc = t // MLSTM_CHUNK

    def chunks(a):
        return jnp.moveaxis(a.reshape(a.shape[:2] + (nc, MLSTM_CHUNK) + a.shape[3:]), 2, 0)

    _, out = lax.scan(mlstm_chunk, state, (chunks(q), chunks(k), chunks(v), chunks(ig), chunks(lf)))
    return jnp.moveaxis(out, 0, 2).reshape(b, h, t, -1)

def mlstm_context_state(k, v, ig, lf):
    b, h, _, dk = k.shape
    C0 = jnp.zeros((b, h, dk, v.shape[-1]), F32_2)
    n0 = jnp.zeros((b, h, dk), F32_2)
    m0 = jnp.zeros((b, h), F32_2)
    return mlstm_state_update(C0, n0, m0, k, v, ig, jnp.cumsum(lf, axis=-1))

def mlstm_mixer(q, k, v, o, ig_f, lf_f, ig_b, lf_b, k_c, v_c, igc_f, lfc_f, igc_b, lfc_b, norm_g):
    H = MLSTM_HEADS
    B_, T_, _ = q.shape
    q = to_heads(q, H).astype(F32_2) * (MLSTM_DQK ** -0.5)
    k = to_heads(k, H).astype(F32_2)
    v = to_heads(v, H).astype(F32_2)
    k_c = to_heads(k_c, H).astype(F32_2)
    v_c = to_heads(v_c, H).astype(F32_2)
    st_f = mlstm_context_state(k_c, v_c, igc_f, lfc_f)
    st_b = mlstm_context_state(jnp.flip(k_c, 2), jnp.flip(v_c, 2), jnp.flip(igc_b, -1), jnp.flip(lfc_b, -1))
    h_f = mlstm_scan(q, k, v, ig_f, lf_f, st_f)
    h_b = jnp.flip(mlstm_scan(jnp.flip(q, 2), jnp.flip(k, 2), jnp.flip(v, 2),
                              jnp.flip(ig_b, -1), jnp.flip(lf_b, -1), st_b), 2)
    h = (h_f + h_b).transpose(0, 2, 1, 3)
    h = rmsnorm(h, norm_g.reshape(H, MLSTM_DV)).reshape(B_, T_, MV)
    return (h * jax.nn.sigmoid(o.astype(F32_2))).astype(o.dtype)

def diff_attention_blocks(q1, q2, k1_all, k2_all, v_all, lam):
    B_, H, T_, d = q1.shape
    nb = T_ // Q_BLOCK
    scale = DIFF_DQK ** -0.5

    def blocks(a):
        return a.reshape(B_, H, nb, Q_BLOCK, d).transpose(2, 0, 1, 3, 4)

    def one_block(qs):
        a1, a2 = qs
        s1 = jnp.einsum('bhqd,bhkd->bhqk', a1, k1_all).astype(F32_2) * scale
        s2 = jnp.einsum('bhqd,bhkd->bhqk', a2, k2_all).astype(F32_2) * scale
        p = jax.nn.softmax(s1, axis=-1) - lam * jax.nn.softmax(s2, axis=-1)
        return jnp.einsum('bhqk,bhkv->bhqv', p.astype(v_all.dtype), v_all)

    out = lax.map(one_block, (blocks(q1), blocks(q2)))
    return out.transpose(1, 2, 0, 3, 4).reshape(B_, H, T_, -1)

def diff_mixer(q, k, v, k_c, v_c, lq1, lk1, lq2, lk2, norm_g, layer_idx):
    H = DIFF_HEADS
    B_, T_, _ = q.shape

    def split_qk(a):
        a = a.reshape(a.shape[0], a.shape[1], H, 2, DIFF_DQK)
        return a[..., 0, :].transpose(0, 2, 1, 3), a[..., 1, :].transpose(0, 2, 1, 3)

    tables = axial_rope_tables(T_)
    q1, q2 = [apply_axial_rope_2(a, tables) for a in split_qk(q)]
    k1, k2 = [apply_axial_rope_2(a, tables) for a in split_qk(k)]
    k1c, k2c = split_qk(k_c)
    k1_all = jnp.concatenate([k1c, k1], axis=2)
    k2_all = jnp.concatenate([k2c, k2], axis=2)
    v_all = jnp.concatenate([to_heads(v_c, H), to_heads(v, H)], axis=2)
    lam_init = 0.8 - 0.6 * math.exp(-0.3 * layer_idx)
    lam = (jnp.exp(jnp.sum(lq1.astype(F32_2) * lk1.astype(F32_2)))
           - jnp.exp(jnp.sum(lq2.astype(F32_2) * lk2.astype(F32_2))) + lam_init)
    o = diff_attention_blocks(q1, q2, k1_all, k2_all, v_all, lam).transpose(0, 2, 1, 3)
    o = rmsnorm(o, norm_g.reshape(H, DIFF_DV)) * (1.0 - lam_init)
    return o.reshape(B_, T_, DVW)

def swiglu(u, w1, w3, w2):
    return (jax.nn.silu(u @ w1) * (u @ w3)) @ w2

def moe_swiglu(u, router_w, w1, w3, w2):
    B_, T_, D = u.shape
    tokens = u.reshape(-1, D)
    N = tokens.shape[0]
    logits = (tokens @ router_w).astype(F32_2)
    top_vals, top_idx = lax.top_k(logits, TOP_K)
    gates = jax.nn.softmax(top_vals, axis=-1)
    A = N * TOP_K
    flat_e = top_idx.reshape(-1)
    flat_tok = jnp.repeat(jnp.arange(N, dtype=jnp.int32), TOP_K)
    flat_g = gates.reshape(-1)
    order = jnp.argsort(flat_e)
    s_e, s_tok, s_g = flat_e[order], flat_tok[order], flat_g[order]
    counts = jnp.bincount(flat_e, length=N_EXPERTS)
    starts = jnp.cumsum(counts) - counts
    padded = ((counts + MOE_BLOCK - 1) // MOE_BLOCK) * MOE_BLOCK
    pends = jnp.cumsum(padded)
    pstarts = pends - padded
    dest = pstarts[s_e] + (jnp.arange(A) - starts[s_e])
    n_blk = (A + MOE_BLOCK - 1) // MOE_BLOCK + N_EXPERTS
    R = n_blk * MOE_BLOCK
    slot_tok = jnp.zeros((R,), jnp.int32).at[dest].set(s_tok)
    slot_g = jnp.zeros((R,), F32_2).at[dest].set(s_g)
    block_e = jnp.clip(jnp.searchsorted(pends, jnp.arange(n_blk) * MOE_BLOCK, side='right'), 0, N_EXPERTS - 1)

    def run_block(args):
        tok_idx, e = args
        xb = tokens[tok_idx]
        return (jax.nn.silu(xb @ w1[e]) * (xb @ w3[e])) @ w2[e]

    y = lax.map(run_block, (slot_tok.reshape(n_blk, MOE_BLOCK), block_e)).reshape(R, D)
    y = y * slot_g[:, None].astype(y.dtype)
    out = jnp.zeros((N, D), y.dtype).at[slot_tok].add(y)
    return out.reshape(B_, T_, D)

def even_layer(x, c, ctx, c_ctx, layer_idx, mod_w, mod_b, mix_pre_g, mix_post_g, w_in, mlstm_gate_b,
               mlstm_conv_w, mlstm_norm_g, lambda_q1, lambda_k1, lambda_q2, lambda_k2, diff_norm_g,
               w_out, ffn_pre_g, ffn_post_g, ffn_w1, ffn_w3, ffn_w2):
    sh_m, sc_m, gt_m, sh_f, sc_f, gt_f = jnp.split(adaln(c, mod_w, mod_b)[:, None, :], 6, axis=-1)
    sh_c, sc_c = jnp.split(adaln(c_ctx, mod_w, mod_b), 6, axis=-1)[:2]
    u = modulate(x, mix_pre_g, sh_m, sc_m)
    p = u @ w_in
    q_m = jax.nn.silu(depthwise_conv(p[..., OFF_MQ:OFF_MK], mlstm_conv_w[:, :MQK]))
    k_m = jax.nn.silu(depthwise_conv(p[..., OFF_MK:OFF_MV], mlstm_conv_w[:, MQK:]))
    v_m = p[..., OFF_MV:OFF_MO]
    o_m = p[..., OFF_MO:OFF_MG]
    ig_f, lf_f, ig_b, lf_b = mlstm_gates(p[..., OFF_MG:OFF_DQ], mlstm_gate_b)
    uc = modulate(ctx, mix_pre_g, sh_c, sc_c)
    kv_mc = uc @ w_in[:, OFF_MK:OFF_MO]
    k_mc = jax.nn.silu(depthwise_conv(kv_mc[..., :MQK], mlstm_conv_w[:, MQK:]))
    v_mc = kv_mc[..., MQK:]
    igc_f, lfc_f, igc_b, lfc_b = mlstm_gates(uc @ w_in[:, OFF_MG:OFF_DQ], mlstm_gate_b)
    kv_dc = uc @ w_in[:, OFF_DK:]
    h_m = mlstm_mixer(q_m, k_m, v_m, o_m, ig_f, lf_f, ig_b, lf_b,
                      k_mc, v_mc, igc_f, lfc_f, igc_b, lfc_b, mlstm_norm_g)
    h_d = diff_mixer(p[..., OFF_DQ:OFF_DK], p[..., OFF_DK:OFF_DV], p[..., OFF_DV:],
                     kv_dc[..., :DQK], kv_dc[..., DQK:],
                     lambda_q1, lambda_k1, lambda_q2, lambda_k2, diff_norm_g, layer_idx)
    mix = jnp.concatenate([h_m, h_d], axis=-1) @ w_out
    x = x + gt_m * rmsnorm(mix, mix_post_g)
    y = swiglu(modulate(x, ffn_pre_g, sh_f, sc_f), ffn_w1, ffn_w3, ffn_w2)
    return x + gt_f * rmsnorm(y, ffn_post_g)

def odd_layer(x, c, mod_w, mod_b, mix_pre_g, mix_post_g, pw1_w, pw1_b, dw_w, dw_b, ln_g, ln_b,
              pw2_w, pw2_b, ffn_pre_g, ffn_post_g, router_w, moe_w1, moe_w3, moe_w2):
    sh_m, sc_m, gt_m, sh_f, sc_f, gt_f = jnp.split(adaln(c, mod_w, mod_b)[:, None, :], 6, axis=-1)
    u = modulate(x, mix_pre_g, sh_m, sc_m)
    a, g = jnp.split(u @ pw1_w + pw1_b, 2, axis=-1)
    h = a * jax.nn.sigmoid(g)
    h = depthwise_conv(h, dw_w) + dw_b
    h = jax.nn.silu(layernorm(h, ln_g, ln_b))
    y = h @ pw2_w + pw2_b
    x = x + gt_m * rmsnorm(y, mix_post_g)
    y = moe_swiglu(modulate(x, ffn_pre_g, sh_f, sc_f), router_w, moe_w1, moe_w3, moe_w2)
    return x + gt_f * rmsnorm(y, ffn_post_g)

def second_inputs(seed: int = 0) -> dict:
    key = jax.random.key(seed)
    keys = list(jax.random.split(key, 48))
    D = D_MODEL

    def nrm(shape, scale):
        return jax.random.normal(keys.pop(), shape, F32_2) * scale

    def gain(n):
        return 1.0 + nrm((n,), 0.05)

    inp = {}
    inp['x'] = nrm((BATCH, SEQ, D), 1.0)
    inp['c'] = nrm((BATCH, D), 1.0)
    inp['ctx'] = nrm((BATCH, CTX_LEN, D), 1.0)
    inp['c_ctx'] = nrm((D,), 1.0)
    inp['l0_mod_w'] = nrm((D, 6 * D), 0.5 * D ** -0.5)
    inp['l0_mod_b'] = nrm((6 * D,), 0.02)
    inp['l0_mix_pre_g'] = gain(D)
    inp['l0_mix_post_g'] = gain(D)
    inp['l0_w_in'] = nrm((D, IN0_WIDTH), D ** -0.5)
    gate_offsets = jnp.concatenate([
        jnp.full((MLSTM_HEADS,), -1.0, F32_2), jnp.linspace(3.0, 6.0, MLSTM_HEADS, dtype=F32_2),
        jnp.full((MLSTM_HEADS,), -1.0, F32_2), jnp.linspace(3.0, 6.0, MLSTM_HEADS, dtype=F32_2)])
    inp['l0_mlstm_gate_b'] = gate_offsets + nrm((MG,), 0.1)
    inp['l0_mlstm_conv_w'] = nrm((MLSTM_CONV, 2 * MQK), MLSTM_CONV ** -0.5)
    inp['l0_mlstm_norm_g'] = gain(MV)
    inp['l0_lambda_q1'] = nrm((DIFF_DQK,), 0.1)
    inp['l0_lambda_k1'] = nrm((DIFF_DQK,), 0.1)
    inp['l0_lambda_q2'] = nrm((DIFF_DQK,), 0.1)
    inp['l0_lambda_k2'] = nrm((DIFF_DQK,), 0.1)
    inp['l0_diff_norm_g'] = gain(DVW)
    inp['l0_w_out'] = nrm((MIX0_WIDTH, D), MIX0_WIDTH ** -0.5)
    inp['l0_ffn_pre_g'] = gain(D)
    inp['l0_ffn_post_g'] = gain(D)
    inp['l0_ffn_w1'] = nrm((D, D_FF), D ** -0.5)
    inp['l0_ffn_w3'] = nrm((D, D_FF), D ** -0.5)
    inp['l0_ffn_w2'] = nrm((D_FF, D), D_FF ** -0.5)
    inp['l1_mod_w'] = nrm((D, 6 * D), 0.5 * D ** -0.5)
    inp['l1_mod_b'] = nrm((6 * D,), 0.02)
    inp['l1_mix_pre_g'] = gain(D)
    inp['l1_mix_post_g'] = gain(D)
    inp['l1_conv_pw1_w'] = nrm((D, 2 * D), D ** -0.5)
    inp['l1_conv_pw1_b'] = nrm((2 * D,), 0.02)
    inp['l1_conv_dw_w'] = nrm((CONV_WIDTH, D), CONV_WIDTH ** -0.5)
    inp['l1_conv_dw_b'] = nrm((D,), 0.02)
    inp['l1_conv_ln_g'] = gain(D)
    inp['l1_conv_ln_b'] = nrm((D,), 0.02)
    inp['l1_conv_pw2_w'] = nrm((D, D), D ** -0.5)
    inp['l1_conv_pw2_b'] = nrm((D,), 0.02)
    inp['l1_ffn_pre_g'] = gain(D)
    inp['l1_ffn_post_g'] = gain(D)
    inp['l1_router_w'] = nrm((D, N_EXPERTS), D ** -0.5)
    inp['l1_moe_w1'] = nrm((N_EXPERTS, D, D_FF_EXPERT), D ** -0.5)
    inp['l1_moe_w3'] = nrm((N_EXPERTS, D, D_FF_EXPERT), D ** -0.5)
    inp['l1_moe_w2'] = nrm((N_EXPERTS, D_FF_EXPERT, D), D_FF_EXPERT ** -0.5)
    return inp

def second_block(x, c, ctx, c_ctx,
              l0_mod_w, l0_mod_b, l0_mix_pre_g, l0_mix_post_g, l0_w_in, l0_mlstm_gate_b,
              l0_mlstm_conv_w, l0_mlstm_norm_g, l0_lambda_q1, l0_lambda_k1, l0_lambda_q2,
              l0_lambda_k2, l0_diff_norm_g, l0_w_out, l0_ffn_pre_g, l0_ffn_post_g,
              l0_ffn_w1, l0_ffn_w3, l0_ffn_w2,
              l1_mod_w, l1_mod_b, l1_mix_pre_g, l1_mix_post_g, l1_conv_pw1_w, l1_conv_pw1_b,
              l1_conv_dw_w, l1_conv_dw_b, l1_conv_ln_g, l1_conv_ln_b, l1_conv_pw2_w,
              l1_conv_pw2_b, l1_ffn_pre_g, l1_ffn_post_g, l1_router_w, l1_moe_w1, l1_moe_w3,
              l1_moe_w2):
    layer_params = (
        (l0_mod_w, l0_mod_b, l0_mix_pre_g, l0_mix_post_g, l0_w_in, l0_mlstm_gate_b,
         l0_mlstm_conv_w, l0_mlstm_norm_g, l0_lambda_q1, l0_lambda_k1, l0_lambda_q2,
         l0_lambda_k2, l0_diff_norm_g, l0_w_out, l0_ffn_pre_g, l0_ffn_post_g,
         l0_ffn_w1, l0_ffn_w3, l0_ffn_w2),
        (l1_mod_w, l1_mod_b, l1_mix_pre_g, l1_mix_post_g, l1_conv_pw1_w, l1_conv_pw1_b,
         l1_conv_dw_w, l1_conv_dw_b, l1_conv_ln_g, l1_conv_ln_b, l1_conv_pw2_w,
         l1_conv_pw2_b, l1_ffn_pre_g, l1_ffn_post_g, l1_router_w, l1_moe_w1, l1_moe_w3,
         l1_moe_w2),
    )
    for layer in range(DEPTH):
        if layer % 2 == 0:
            x = even_layer(x, c, ctx, c_ctx, layer, *layer_params[layer])
        else:
            x = odd_layer(x, c, *layer_params[layer])
    return x


def setup_inputs(seed=0):
    out = dict(first_inputs(seed))
    for name, value in second_inputs(seed + 1).items():
        if name != "x":
            out[name + "_2"] = value
    return out


def reference(
    x, c, ctx, c_ctx, norm_g, ada_w, ada_b, dn_w_in, dn_conv_w, dn_a_log, dn_dt_bias,
    dn_o_norm_g, dn_w_out, att_w_in, att_q_norm_g, att_k_norm_g, att_w_out, final_norm_g, c_2,
    ctx_2, c_ctx_2, l0_mod_w_2, l0_mod_b_2, l0_mix_pre_g_2, l0_mix_post_g_2, l0_w_in_2,
    l0_mlstm_gate_b_2, l0_mlstm_conv_w_2, l0_mlstm_norm_g_2, l0_lambda_q1_2, l0_lambda_k1_2,
    l0_lambda_q2_2, l0_lambda_k2_2, l0_diff_norm_g_2, l0_w_out_2, l0_ffn_pre_g_2,
    l0_ffn_post_g_2, l0_ffn_w1_2, l0_ffn_w3_2, l0_ffn_w2_2, l1_mod_w_2, l1_mod_b_2,
    l1_mix_pre_g_2, l1_mix_post_g_2, l1_conv_pw1_w_2, l1_conv_pw1_b_2, l1_conv_dw_w_2,
    l1_conv_dw_b_2, l1_conv_ln_g_2, l1_conv_ln_b_2, l1_conv_pw2_w_2, l1_conv_pw2_b_2,
    l1_ffn_pre_g_2, l1_ffn_post_g_2, l1_router_w_2, l1_moe_w1_2, l1_moe_w3_2, l1_moe_w2_2,
):
    x = first_block(
        x, c, ctx, c_ctx, norm_g, ada_w, ada_b, dn_w_in, dn_conv_w, dn_a_log, dn_dt_bias,
        dn_o_norm_g, dn_w_out, att_w_in, att_q_norm_g, att_k_norm_g, att_w_out, final_norm_g,
    )
    return second_block(
        x, c_2, ctx_2, c_ctx_2, l0_mod_w_2, l0_mod_b_2, l0_mix_pre_g_2, l0_mix_post_g_2,
        l0_w_in_2, l0_mlstm_gate_b_2, l0_mlstm_conv_w_2, l0_mlstm_norm_g_2, l0_lambda_q1_2,
        l0_lambda_k1_2, l0_lambda_q2_2, l0_lambda_k2_2, l0_diff_norm_g_2, l0_w_out_2,
        l0_ffn_pre_g_2, l0_ffn_post_g_2, l0_ffn_w1_2, l0_ffn_w3_2, l0_ffn_w2_2, l1_mod_w_2,
        l1_mod_b_2, l1_mix_pre_g_2, l1_mix_post_g_2, l1_conv_pw1_w_2, l1_conv_pw1_b_2,
        l1_conv_dw_w_2, l1_conv_dw_b_2, l1_conv_ln_g_2, l1_conv_ln_b_2, l1_conv_pw2_w_2,
        l1_conv_pw2_b_2, l1_ffn_pre_g_2, l1_ffn_post_g_2, l1_router_w_2, l1_moe_w1_2,
        l1_moe_w3_2, l1_moe_w2_2,
    )


_drawn_inputs = setup_inputs


def setup_inputs(seed=0):
    import zlib

    import numpy as np

    out = dict(_drawn_inputs(seed))
    spreads = {}
    factors = {'norm_g': 3.468,
     'dn_o_norm_g': 4.094,
     'att_q_norm_g': 8.0,
     'att_k_norm_g': 8.0,
     'l0_mix_pre_g_2': 2.915,
     'l0_mlstm_norm_g_2': 4.206,
     'l0_lambda_q1_2': 3.847,
     'l0_lambda_k1_2': 6.176,
     'l0_diff_norm_g_2': 3.562,
     'l1_mix_pre_g_2': 2.953,
     'l1_mix_post_g_2': 3.311,
     'l1_conv_pw1_b_2': 5.184,
     'l1_conv_dw_b_2': 2.845,
     'l1_conv_ln_b_2': 5.838,
     'l1_conv_pw2_b_2': 4.157,
     'l1_ffn_post_g_2': 4.355}
    for name, (base, spread) in spreads.items():
        noise = np.random.default_rng([zlib.crc32(name.encode()), seed]).standard_normal(out[name].shape)
        drawn = base * np.exp(spread * noise) if base else spread * noise
        out[name] = jnp.asarray(drawn.astype(out[name].dtype))
    for name, factor in factors.items():
        out[name] = (out[name] * factor).astype(out[name].dtype)
    return out
```

```python
from contextlib import ExitStack
from collections import namedtuple

import numpy as np
import concourse.bass as bass
from concourse import mybir
from concourse.alu_op_type import AluOpType as ALU

FP32 = mybir.dt.float32
U32 = mybir.dt.uint32
ACT = mybir.ActivationFunctionType
AX = mybir.AxisListType.X

P = 128
D = 1024
KT = D // P
LAT = 512
CTX = 256
TOK = CTX + LAT
NC6 = TOK // P
EPS = 1e-6
BANK = 512

DN_GROUPS = 8
DN_TILES = 6
DN_CONVS = 4
DN_K = 5
DN_GAP = 4
DN_RAW = TOK + 2 * DN_GAP
DN_CONV = TOK + DN_GAP
DN_PAIRS = 3
LEVELS = 7
FORWARD = [0, 1, 2, 3, 4, 5]
BACKWARD = [1, 0, 5, 4, 3, 2]
ORDERS = (FORWARD, BACKWARD)


def first_seen(direction, chunk):
    return ORDERS[direction].index(chunk) < ORDERS[1 - direction].index(chunk)


def spans_of(n):
    return [(0, CTX), (CTX, LAT)] if n == TOK else [(0, LAT)]


class Smalls:

    def __init__(self):
        self.at, self.width, self.parts = {}, 0, []

    def put(self, name, array):
        array = np.asarray(array, np.float32)
        array = array.reshape(array.shape[0], -1)
        assert array.shape[0] == P
        self.at[name] = (self.width, array.shape[1])
        self.parts.append(array)
        self.width += array.shape[1]

    def packed(self):
        return np.ascontiguousarray(np.concatenate(self.parts, axis=1))


def columns(vector):
    return np.asarray(vector, np.float32).reshape(-1, P).T


def on_all(row):
    row = np.asarray(row, np.float32).reshape(1, -1)
    return np.repeat(row, P, axis=0)


def tiles(w):
    k, n = w.shape
    return np.ascontiguousarray(w.reshape(k // P, P, n // P, P).transpose(2, 1, 0, 3)).reshape(n // P, P, k)


def rows(w):
    k, n = w.shape
    return np.ascontiguousarray(w.reshape(k // P, P, n).transpose(1, 0, 2)).reshape(P, -1)



def load_once(k, h):
    nc = k.nc
    with ExitStack() as c:
        loaded = c.enter_context(nc.semaphore("loaded"))
        block = c.enter_context(nc.Block())

        @block.sync
        def _(sp):
            sp.dma_start(k.small[:, :], k.io["smalls"]).then_inc(loaded, 16)
            sp.dma_start(k.const[:, :], k.io["consts"]).then_inc(loaded, 16)
            sp.dma_start(h[:, :, :], k.io["tokens"]).then_inc(loaded, 16)
            sp.wait_ge(loaded, 48)


def recycle(k):
    nc = k.nc
    ids = sorted(nc.released_uncleared_semaphores)
    with nc.Block() as block:

        @block.gpsimd
        def _(pool):
            first = 0
            for i in range(1, len(ids) + 1):
                if i == len(ids) or ids[i] != ids[i - 1] + 1:
                    pool.sem_clear(range(ids[first], ids[i - 1] + 1))
                    first = i


def load(k, name, dst, src):
    nc = k.nc
    with ExitStack() as c:
        loaded = c.enter_context(nc.semaphore(f"{name}_loaded"))
        block = c.enter_context(nc.Block())

        @block.sync
        def _(sp):
            sp.dma_start(dst, k.io[src]).then_inc(loaded, 16)
            sp.wait_ge(loaded, 16)


def store(k, name, src):
    nc = k.nc
    with ExitStack() as c:
        stored = c.enter_context(nc.semaphore(f"{name}_stored"))
        block = c.enter_context(nc.Block())

        @block.sync
        def _(sp):
            sp.dma_start(k.io["out"], src).then_inc(stored, 16)
            sp.wait_ge(stored, 16)


MOD_TILES = 144
MOD_SLOTS = 3
MOD_AT_ONCE = 4
CONDS = 4


def modulations(k):
    nc = k.nc
    rounds = MOD_TILES // (MOD_SLOTS * MOD_AT_ONCE)
    with ExitStack() as c:
        sem = lambda n: c.enter_context(nc.semaphore(n))
        ring = c.enter_context(nc.sbuf_tensor("mod_ring", [P, MOD_SLOTS, KT, BANK], FP32))
        cond = c.enter_context(nc.sbuf_tensor("mod_cond", [P, KT, CONDS], FP32))
        row = c.enter_context(nc.sbuf_tensor("mod_row", [P, MOD_SLOTS, BANK], FP32))
        w_ready = [sem(f"mod_w_ready{s}") for s in range(MOD_SLOTS)]
        cond_ready, group_done, row_ready = sem("mod_cond_ready"), sem("mod_group_done"), sem("mod_row_ready")
        turned, taken = sem("mod_turned"), sem("mod_taken")
        block = c.enter_context(nc.Block())
        w = k.io["mod_w"]

        @block.sync
        def _(sp):
            for s in range(MOD_SLOTS):
                sp.dma_start(ring[:, s, :, :], w[s]).then_inc(w_ready[s], 16)
            with sp.Fori(1, rounds) as r:
                for s in range(MOD_SLOTS):
                    sp.wait_ge(group_done, r * MOD_SLOTS + (s + 1 - MOD_SLOTS))
                    sp.dma_start(ring[:, s, :, :], w[r * MOD_SLOTS + s]).then_inc(w_ready[s], 16)

        @block.scalar
        def _(act):
            nc.scalar.activation(cond[:, :, :].rearrange("p a b -> p (a b)"), k.vec("conds"),
                                 ACT.Silu).then_inc(cond_ready, 1)
            with act.Fori(0, rounds) as r:
                for s in range(MOD_SLOTS):
                    act.wait_ge(group_done, r * MOD_SLOTS + (s + 1))
                    act.wait_ge(turned, r * MOD_SLOTS)
                    nc.scalar.activation(row[0:CONDS, s, :], k.ps[0:CONDS, s, :], ACT.Copy).then_inc(row_ready, 1)

        @block.tensor
        def _(pe):
            pe.wait_ge(cond_ready, 1)
            with pe.Fori(0, rounds) as r:
                def turn(s):
                    pe.wait_ge(row_ready, r * MOD_SLOTS + (s + 1))
                    pe.wait_ge(taken, r * MOD_SLOTS)
                    for t in range(MOD_AT_ONCE):
                        last = nc.tensor.matmul(k.ps[:, MOD_SLOTS + s, t * CONDS:(t + 1) * CONDS], row[0:CONDS, s, t * P:(t + 1) * P],
                                                k.ident[0:CONDS, 0:CONDS], start=True, stop=True)
                    last.then_inc(turned, 1)

                for s in range(MOD_SLOTS):
                    pe.wait_ge(w_ready[s], r * 16 + 16)
                    pe.wait_ge(row_ready, r * MOD_SLOTS)
                    for kt in range(KT):
                        last = nc.tensor.matmul(k.ps[0:CONDS, s, :], cond[:, kt, :], ring[:, s, kt, :],
                                                start=(kt == 0), stop=(kt == KT - 1))
                    last.then_inc(group_done, 1)
                    if s:
                        turn(s - 1)
                turn(MOD_SLOTS - 1)

        @block.vector
        def _(dve):
            with dve.Fori(0, rounds) as r:
                for s in range(MOD_SLOTS):
                    dve.wait_ge(turned, r * MOD_SLOTS + (s + 1))
                    at = bass.ds(r * (MOD_SLOTS * MOD_AT_ONCE) + s * MOD_AT_ONCE, MOD_AT_ONCE)
                    nc.vector.tensor_tensor(k.mod[:, at, :],
                                            k.ps[:, MOD_SLOTS + s, 0:MOD_AT_ONCE * CONDS].rearrange("p (t n) -> p t n", n=CONDS),
                                            k.vec("mod_b")[:, at].unsqueeze(2).broadcast_to([P, MOD_AT_ONCE, CONDS]),
                                            ALU.add).then_inc(taken, 1)
            dve.wait_ge(taken, MOD_TILES // MOD_AT_ONCE)


def norm_modulate(k, name, src, dst, ntok, gain, parts):
    nc = k.nc
    with ExitStack() as c:
        sem = lambda n: c.enter_context(nc.semaphore(f"{name}_{n}"))
        sq = c.enter_context(nc.sbuf_tensor(f"{name}_sq", [P, 2, ntok], FP32))
        inv = c.enter_context(nc.sbuf_tensor(f"{name}_inv", [P, ntok], FP32))
        g = c.enter_context(nc.sbuf_tensor(f"{name}_g", [P, len(parts), KT], FP32))
        squared, summed, log_ready, inv_ready = sem("squared"), sem("summed"), sem("log"), sem("inv")
        gain_ready, scaled, out_ready = sem("gain"), sem("scaled"), sem("out")
        block = c.enter_context(nc.Block())
        banks = [(b, t0, n) for b, (t0, n, _, _) in enumerate(parts)]

        @block.scalar
        def _(act):
            for kt in range(KT):
                if kt >= 2:
                    act.wait_ge(summed, kt - 1)
                nc.scalar.activation(sq[:, kt % 2, :], src[:, kt, 0:ntok], ACT.Square).then_inc(squared, 1)
            act.wait_ge(summed, KT)
            for b, t0, n in banks:
                last = nc.scalar.activation(inv[:, t0:t0 + n], k.ps[:, b, 0:n], ACT.Ln, bias=k.eps, scale=1.0 / D)
            last.then_inc(log_ready, 1)
            act.wait_ge(log_ready, 1)
            nc.scalar.activation(inv[:, :], inv[:, :], ACT.Exp, scale=-0.5).then_inc(inv_ready, 1)
            for kt in range(KT):
                act.wait_ge(scaled, kt + 1)
                for b, (t0, n, _, shift) in enumerate(parts):
                    last = nc.scalar.activation(dst[:, kt, t0:t0 + n], dst[:, kt, t0:t0 + n], ACT.Identity,
                                                scale=g[:, b, kt:kt + 1], bias=shift[:, kt:kt + 1])
                last.then_inc(out_ready, 1)
            act.wait_ge(out_ready, KT)

        @block.tensor
        def _(pe):
            for kt in range(KT):
                pe.wait_ge(squared, kt + 1)
                for b, t0, n in banks:
                    last = nc.tensor.matmul(k.ps[:, b, 0:n], k.ones, sq[:, kt % 2, t0:t0 + n],
                                            start=(kt == 0), stop=(kt == KT - 1))
                last.then_inc(summed, 1)

        @block.vector
        def _(dve):
            for b, (_, _, scale, _) in enumerate(parts):
                last = nc.vector.scalar_tensor_tensor(g[:, b, :], scale, 1.0, gain, ALU.add, ALU.mult)
            last.then_inc(gain_ready, 1)
            dve.wait_ge(gain_ready, 1)
            dve.wait_ge(inv_ready, 1)
            for kt in range(KT):
                nc.vector.tensor_tensor(dst[:, kt, 0:ntok], src[:, kt, 0:ntok], inv[:, :], ALU.mult).then_inc(scaled, 1)
            dve.wait_ge(scaled, KT)


def norm_residual(k, name, h, y, gain, gate):
    nc = k.nc
    with ExitStack() as c:
        sem = lambda n: c.enter_context(nc.semaphore(f"{name}_{n}"))
        sq = c.enter_context(nc.sbuf_tensor(f"{name}_sq", [P, 2, LAT], FP32))
        inv = c.enter_context(nc.sbuf_tensor(f"{name}_inv", [P, LAT], FP32))
        g = c.enter_context(nc.sbuf_tensor(f"{name}_g", [P, KT], FP32))
        squared, summed, log_ready, inv_ready = sem("squared"), sem("summed"), sem("log"), sem("inv")
        gain_ready, scaled, out_ready = sem("gain"), sem("scaled"), sem("out")
        block = c.enter_context(nc.Block())

        @block.scalar
        def _(act):
            for kt in range(KT):
                if kt >= 2:
                    act.wait_ge(summed, kt - 1)
                nc.scalar.activation(sq[:, kt % 2, :], y[:, kt, :], ACT.Square).then_inc(squared, 1)
            act.wait_ge(summed, KT)
            nc.scalar.activation(inv[:, :], k.ps[:, 0, :], ACT.Ln, bias=k.eps, scale=1.0 / D).then_inc(log_ready, 1)
            act.wait_ge(log_ready, 1)
            nc.scalar.activation(inv[:, :], inv[:, :], ACT.Exp, scale=-0.5).then_inc(inv_ready, 1)

        @block.tensor
        def _(pe):
            for kt in range(KT):
                pe.wait_ge(squared, kt + 1)
                nc.tensor.matmul(k.ps[:, 0, :], k.ones, sq[:, kt % 2, :],
                                 start=(kt == 0), stop=(kt == KT - 1)).then_inc(summed, 1)

        @block.vector
        def _(dve):
            if gate is None:
                nc.vector.tensor_copy(g[:, :], gain).then_inc(gain_ready, 1)
            else:
                nc.vector.tensor_tensor(g[:, :], gate, gain, ALU.mult).then_inc(gain_ready, 1)
            dve.wait_ge(gain_ready, 1)
            dve.wait_ge(inv_ready, 1)
            for kt in range(KT):
                last = nc.vector.tensor_tensor(y[:, kt, :], y[:, kt, :], inv[:, :], ALU.mult)
            last.then_inc(scaled, 1)
            dve.wait_ge(scaled, 1)
            for kt in range(KT):
                if h is None:
                    last = nc.vector.tensor_scalar(y[:, kt, :], y[:, kt, :], g[:, kt:kt + 1], None, ALU.mult)
                else:
                    last = nc.vector.scalar_tensor_tensor(h[:, kt, :], y[:, kt, :], g[:, kt:kt + 1], h[:, kt, :],
                                                          ALU.mult, ALU.add)
            last.then_inc(out_ready, 1)
            dve.wait_ge(out_ready, 1)


def linear(k, name, w, src, kt_n, nt, spans, evacuate, unroll=2, on="vector", extra=None):
    nc = k.nc
    rounds = nt // unroll
    assert rounds * unroll == nt and unroll * len(spans) <= 8
    with ExitStack() as c:
        sem = lambda n: c.enter_context(nc.semaphore(f"{name}_{n}"))
        ring = c.enter_context(nc.sbuf_tensor(f"{name}_ring", [P, unroll, kt_n * P], FP32))
        w_ready = [sem(f"w_ready{s}") for s in range(unroll)]
        tile_done, taken = sem("tile_done"), sem("taken")
        block = c.enter_context(nc.Block())

        @block.sync
        def _(sp):
            for s in range(unroll):
                sp.dma_start(ring[:, s, :], w[s]).then_inc(w_ready[s], 16)
            if rounds > 1:
                with sp.Fori(1, rounds) as r:
                    for s in range(unroll):
                        sp.wait_ge(tile_done, r * unroll + (s + 1 - unroll))
                        sp.dma_start(ring[:, s, :], w[r * unroll + s]).then_inc(w_ready[s], 16)

        @block.tensor
        def _(pe):
            with pe.Fori(0, rounds) as r:
                for s in range(unroll):
                    pe.wait_ge(w_ready[s], r * 16 + 16)
                    pe.wait_ge(taken, r * unroll)
                    for kt in range(kt_n):
                        for b, (t0, n) in enumerate(spans):
                            last = nc.tensor.matmul(k.ps[:, s * len(spans) + b, 0:n], ring[:, s, kt * P:(kt + 1) * P],
                                                    src(kt, t0, n), start=(kt == 0), stop=(kt == kt_n - 1))
                    last.then_inc(tile_done, 1)

        def take(eng):
            with eng.Fori(0, rounds) as r:
                for s in range(unroll):
                    eng.wait_ge(tile_done, r * unroll + (s + 1))
                    evacuate(r * unroll + s, s, [k.ps[:, s * len(spans) + b, 0:n] for b, (_, n) in enumerate(spans)]).then_inc(taken, 1)
            eng.wait_ge(taken, nt)

        block.vector(take) if on == "vector" else block.scalar(take)


def delta_gates(k, u):
    nc = k.nc
    n_heads = 2 * DN_GROUPS
    with ExitStack() as c:
        sem = lambda n: c.enter_context(nc.semaphore(f"dng_{n}"))
        sb = lambda n, s: c.enter_context(nc.sbuf_tensor(f"dng_{n}", s, FP32))
        w = sb("w", [P, KT, 64])
        lin, mag = sb("lin", [P, 2 * n_heads, NC6]), sb("mag", [P, 2 * n_heads, NC6])
        neg_a = sb("neg_a", [P, 2 * n_heads])
        g = sb("g", [P, 2 * n_heads, NC6])
        gc = sb("gc", [P, 2 * n_heads, NC6])
        w_ready, projected, lin_ready, mag_ready = sem("w"), sem("projected"), sem("lin"), sem("mag")
        exp_ready, log_ready, sp_ready, g_ready, summed = sem("exp"), sem("log"), sem("sp"), sem("g"), sem("summed")
        beta_ready, nega_ready, gc_ready, stored = sem("beta"), sem("nega"), sem("gc"), sem("stored")
        block = c.enter_context(nc.Block())
        ab = k.ps[:, 0, 0:NC6 * 64].rearrange("p (c q n) -> p q n c", c=NC6, q=2)
        gate = k.dn_gate

        def put(q, d):
            return gate[:, :, q, d, :, :].rearrange("p g c v -> p g v c")

        def heads(t, d):
            return t[:, d * n_heads:(d + 1) * n_heads, :].rearrange("p (g v) c -> p g v c", v=2)

        @block.sync
        def _(sp):
            sp.dma_start(w[:, :, :].rearrange("p a b -> p (a b)"), k.io["dn_w_ab"]).then_inc(w_ready, 16)

        @block.tensor
        def _(pe):
            pe.wait_ge(w_ready, 16)
            for ch in range(NC6):
                for kt in range(KT):
                    last = nc.tensor.matmul(k.ps[:, 0, ch * 64:(ch + 1) * 64], u[:, kt, ch * P:(ch + 1) * P],
                                            w[:, kt, :], start=(kt == 0), stop=(kt == KT - 1))
            last.then_inc(projected, 1)
            pe.wait_ge(g_ready, 1)
            for d in range(2):
                last = nc.tensor.matmul(k.ps[:, 1 + d, 0:n_heads * NC6], k.tri[d],
                                        g[:, d * n_heads:(d + 1) * n_heads, :].rearrange("p h c -> p (h c)"),
                                        start=True, stop=True)
            last.then_inc(summed, 1)

        @block.vector
        def _(dve):
            dve.wait_ge(projected, 1)
            nc.vector.tensor_tensor(lin[:, :, :], ab[:, 1, :, :],
                                    k.vec("dn_dt").unsqueeze(2).broadcast_to([P, 2 * n_heads, NC6]), ALU.add).then_inc(lin_ready, 1)
            dve.wait_ge(lin_ready, 1)
            nc.vector.scalar_tensor_tensor(mag[:, :, :], lin[:, :, :], -1.0, lin[:, :, :], ALU.mult, ALU.max).then_inc(mag_ready, 1)
            dve.wait_ge(log_ready, 1)
            nc.vector.scalar_tensor_tensor(lin[:, :, :], lin[:, :, :], 0.0, mag[:, :, :], ALU.max, ALU.add).then_inc(sp_ready, 1)
            dve.wait_ge(sp_ready, 1)
            dve.wait_ge(nega_ready, 1)
            nc.vector.scalar_tensor_tensor(g[:, :, :], lin[:, :, :], -1.0,
                                           neg_a[:, :].unsqueeze(2).broadcast_to([P, 2 * n_heads, NC6]),
                                           ALU.mult, ALU.mult).then_inc(g_ready, 1)
            dve.wait_ge(g_ready, 1)
            dve.wait_ge(summed, 1)
            for d in range(2):
                last = nc.vector.tensor_copy(gc[:, d * n_heads:(d + 1) * n_heads, :].rearrange("p h c -> p (h c)"),
                                             k.ps[:, 1 + d, 0:n_heads * NC6])
            last.then_inc(gc_ready, 1)
            dve.wait_ge(gc_ready, 1)
            for d in range(2):
                nc.vector.tensor_copy(put(0, d), heads(g, d))
                last = nc.vector.tensor_copy(put(1, d), heads(gc, d))
            last.then_inc(stored, 1)
            dve.wait_ge(beta_ready, 1)
            for d in range(2):
                nc.vector.tensor_scalar(put(2, d), heads(lin, d), -1.0, None, ALU.mult)
                last = nc.vector.tensor_copy(put(3, d), heads(mag, d))
            last.then_inc(stored, 1)
            dve.wait_ge(stored, 2)

        @block.scalar
        def _(act):
            nc.scalar.activation(neg_a[:, :], k.vec("dn_a_log"), ACT.Exp).then_inc(nega_ready, 1)
            act.wait_ge(mag_ready, 1)
            nc.scalar.activation(mag[:, :, :], mag[:, :, :], ACT.Exp, scale=-1.0).then_inc(exp_ready, 1)
            act.wait_ge(exp_ready, 1)
            nc.scalar.activation(mag[:, :, :], mag[:, :, :], ACT.Ln, bias=1.0).then_inc(log_ready, 1)
            act.wait_ge(gc_ready, 1)
            nc.scalar.activation(lin[:, :, :], gc[:, :, :], ACT.Exp)
            nc.scalar.activation(mag[:, :, :], ab[:, 0, :, :], ACT.Sigmoid).then_inc(beta_ready, 1)


def conv_at(chunk):
    return chunk * P if chunk < 2 else CTX + DN_GAP + (chunk - 2) * P


def delta_rule(k, u, og):
    nc = k.nc
    with ExitStack() as c:
        sem = lambda n: c.enter_context(nc.semaphore(f"dn_{n}"))
        sb = lambda n, s: c.enter_context(nc.sbuf_tensor(f"dn_{n}", s, FP32))
        RING = 3
        ring = sb("ring", [P, RING, D])
        raw = sb("raw", [P, DN_CONVS, DN_RAW])
        acc = sb("acc", [P, 2, DN_CONV])
        qk = sb("qk", [P, 2, DN_CONV])
        vf = sb("vf", [P, 2, DN_CONV])
        ktok = sb("ktok", [P, NC6, P])
        vtok = sb("vtok", [P, NC6, 2, P])
        qkm = sb("qkm", [P, NC6, 2, 2, P])
        gs = sb("gs", [P, 4, 2, NC6, 2])
        dec = sb("dec", [P, 8, P])
        eg = sb("eg", [P, 8, P])
        at = sb("at", [P, 8, P])
        qa = sb("qa", [P, 8, P])
        qd = sb("qd", [P, 8, P])
        kd = sb("kd", [P, 8, P])
        mt = sb("mt", [P, 8, P])
        xx = sb("xx", [P, 8, 2, P])
        y = sb("y", [P, 8, P])
        r = sb("r", [P, 4, P])
        vn = sb("vn", [P, 4, P])
        s = sb("s", [P, 2, 2, P])
        o = sb("o", [P, 2, TOK])
        sq = inv = xx[:, :, :, :].rearrange("p n x t -> p (n x t)")[:, 0:2 * DN_CONV].rearrange("p (i n) -> p i n", i=2)

        w_ready = [sem(f"w_ready{i}") for i in range(RING)]
        (pad_ready, tile_done, taken, tap, conv_done, featured, squared, summed, log_ready, inv_ready, normed,
         turned, tok_ready, paired, qkm_ready, gs_ready, state_zero, gcb_ready, diff_ready, dec_ready, eg_ready,
         qa_ready, at_ready, qd_ready, kd_ready, mt_ready, xt_ready, xt_turned, x_ready, y_done, y_ready, p_done,
         xx_ready, ks_done, r_ready, tr_done, vn_ready, o_done, su_done, s_ready, o_ready, osq_ready, osum_done,
         olog_ready, oinv_ready, on_ready, og_ready) = (sem(n) for n in (
            "pad_ready tile_done taken tap conv_done featured squared summed log_ready inv_ready normed "
            "turned tok_ready paired qkm_ready gs_ready state_zero gcb_ready diff_ready dec_ready eg_ready "
            "qa_ready at_ready qd_ready kd_ready mt_ready xt_ready xt_turned x_ready y_done y_ready p_done "
            "xx_ready ks_done r_ready tr_done vn_ready o_done su_done s_ready o_ready osq_ready osum_done "
            "olog_ready oinv_ready on_ready og_ready").split())
        block = c.enter_context(nc.Block())
        w = k.io["dn_w"]

        def chunk_of(pair, n):
            return ORDERS[(n // 2) % 2][2 * pair + n // 4]

        def last_of(direction):
            return P - 1 if direction == 0 else 0

        @block.sync
        def _(sp):
            for i in range(RING):
                sp.dma_start(ring[:, i, :], w[i]).then_inc(w_ready[i], 16)
            n_tiles = DN_GROUPS * DN_TILES
            with sp.Fori(1, n_tiles // RING) as t:
                for i in range(RING):
                    sp.wait_ge(tile_done, t * RING + (i + 1 - RING))
                    sp.dma_start(ring[:, i, :], w[t * RING + i]).then_inc(w_ready[i], 16)

        @block.tensor
        def _(pe):
            def project(g, i, bank, first, last):
                if first == 0:
                    pe.wait_ge(w_ready[i % RING], g * 32 + (16 * (i // RING) + 16))
                for m in range(first, last + 1):
                    kt, b = m // 2, m % 2
                    t0, n = spans_of(TOK)[b]
                    done = nc.tensor.matmul(k.ps[:, bank + b, 0:n], ring[:, i % RING, kt * P:(kt + 1) * P],
                                            u[:, kt, t0:t0 + n], start=(kt == 0), stop=(kt == KT - 1))
                if last == 2 * KT - 1:
                    done.then_inc(tile_done, 1)

            def group(g, is_last):
                pe.wait_ge(olog_ready, g)
                for i in range(2):
                    pe.wait_ge(squared, g * 2 + (i + 1))
                    for b in range(2):
                        last = nc.tensor.matmul(k.ps[:, 4 + 2 * i + b, 0:DN_CONV // 2], k.ones,
                                                sq[:, i, b * (DN_CONV // 2):(b + 1) * (DN_CONV // 2)], start=True, stop=True)
                    last.then_inc(summed, 1)
                pe.wait_ge(taken, g * DN_TILES + DN_CONVS)
                for i in range(3):
                    if i == 2:
                        pe.wait_ge(normed, g * 2 + 2)
                    src = vf[:, i, :] if i < 2 else qk[:, 1, :]
                    if i < 2:
                        pe.wait_ge(featured, g * DN_CONVS + (3 + i))
                    for ch in range(NC6):
                        last = nc.tensor.transpose(k.ps[:, 2 * i + ch // 3, (ch % 3) * P:(ch % 3 + 1) * P],
                                                   src[:, conv_at(ch):conv_at(ch) + P], k.ident)
                    last.then_inc(turned, 1)
                for ch in range(NC6):
                    if ch == 0:
                        pe.wait_ge(tok_ready, g * 3 + 1)
                    if ch == 4:
                        pe.wait_ge(tok_ready, g * 3 + 2)
                    at_c = slice(conv_at(ch), conv_at(ch) + P)
                    b = (0, 0, 1, 1, 2, 2)[ch]
                    nc.tensor.matmul(k.ps[:, b, (ch % 2) * 2 * P:(ch % 2 + 1) * 2 * P], qk[:, 1, at_c], qk[:, :, at_c],
                                     start=True, stop=True).then_inc(paired, 1)
                pe.wait_ge(qkm_ready, g * NC6 + NC6)
                pe.wait_ge(tok_ready, g * 3 + 3)
                pe.wait_ge(gs_ready, g + 1)
                pe.wait_ge(state_zero, g + 1)
                for pair in range(DN_PAIRS):
                    gp = g * DN_PAIRS + pair
                    beside = pair == 0 or not is_last
                    of, tile = (g, DN_CONVS) if pair == 0 else (g + 1, 2 * pair - 2)
                    if pair:
                        pe.wait_ge(o_ready, g * 6 + 2 * pair)
                    for n in range(8):
                        ch, d, v = chunk_of(pair, n), (n // 2) % 2, n % 2
                        last = nc.tensor.matmul(k.ps[:, n // 4, (n % 4) * P:(n % 4 + 1) * P],
                                                gs[:, 0, d, ch, v:v + 1].broadcast_to([P, P]), k.tri[d], start=True, stop=True)
                    last.then_inc(gcb_ready, 1)
                    if beside:
                        project(of, tile, 6, 0, 11)
                    pe.wait_ge(xt_ready, gp + 1)
                    pe.wait_ge(eg_ready, gp + 1)
                    for n in range(8):
                        last = nc.tensor.transpose(k.ps[:, n // 4, (n % 4) * P:(n % 4 + 1) * P], xx[:, n, 1, :], k.ident)
                    last.then_inc(xt_turned, 1)
                    for level in range(1, LEVELS):
                        done = gp * (2 * (LEVELS - 1)) + 2 * (level - 1)
                        for a in range(2):
                            if level == 1:
                                pe.wait_ge(x_ready, gp + 1)
                            else:
                                pe.wait_ge(xx_ready, done + (a - 1))
                            if a == 0:
                                pe.wait_ge(mt_ready, gp * LEVELS + (level + 1))
                            for n in range(4 * a, 4 * a + 4):
                                last = nc.tensor.matmul(k.ps[:, a, (n % 4) * P:(n % 4 + 1) * P], mt[:, n, :], xx[:, n, 0, :],
                                                        start=True, stop=True)
                            last.then_inc(y_done, 1)
                        if beside and level <= 4:
                            project(of, tile, 6, 11 + level, 11 + level)
                        for a in range(2):
                            pe.wait_ge(y_ready, done + (a + 1))
                            if level == 1 and a == 0 and (pair == 1 or pair == 2 and not is_last):
                                pe.wait_ge(taken, g * DN_TILES + (DN_TILES if pair == 1 else DN_TILES + 2))
                            for n in range(4 * a, 4 * a + 4):
                                bank, col = 2 + n // 2, (n % 2) * 2 * P
                                if level < LEVELS - 1:
                                    nc.tensor.matmul(k.ps[:, bank, col:col + P], xx[:, n, 1, :], y[:, n, :], start=True, stop=True)
                                last = nc.tensor.matmul(k.ps[:, bank, col + P:col + 2 * P], y[:, n, :], xx[:, n, 1, :],
                                                        start=True, stop=True)
                            last.then_inc(p_done, 1)
                    pe.wait_ge(qd_ready, gp + 1)
                    pe.wait_ge(kd_ready, gp + 1)
                    if beside:
                        pe.wait_ge(taken, of * DN_TILES + (tile + 1))
                    for a in range(2):
                        step = gp * 2 + a
                        if pair or a:
                            pe.wait_ge(s_ready, g * 6 + (2 * pair + a))
                        for d in range(2):
                            ch = ORDERS[d][2 * pair + a]
                            last = nc.tensor.matmul(k.ps[:, 6, 2 * d * P:(2 * d + 2) * P], qk[:, 1, conv_at(ch):conv_at(ch) + P],
                                                    s[:, d, :, :], start=True, stop=True)
                        last.then_inc(ks_done, 1)
                        if beside:
                            if a == 0:
                                pe.wait_ge(xx_ready, (gp + 1) * 2 * (LEVELS - 1) - 1)
                            project(of, tile + 1, 2, 9 * a, 9 * a + 2)
                        pe.wait_ge(r_ready, step + 1)
                        pe.wait_ge(xx_ready, (gp + 1) * 2 * (LEVELS - 1) - (1 - a))
                        for n in range(4):
                            last = nc.tensor.matmul(k.ps[:, 7, n * P:(n + 1) * P], xx[:, 4 * a + n, 1, :], r[:, n, :],
                                                    start=True, stop=True)
                        last.then_inc(tr_done, 1)
                        if beside:
                            project(of, tile + 1, 2, 9 * a + 3, 9 * a + 5)
                        pe.wait_ge(vn_ready, step + 1)
                        for n in range(4):
                            last = nc.tensor.matmul(k.ps[:, 4 + a, n * P:(n + 1) * P], kd[:, 4 * a + n, :], vn[:, n, :],
                                                    start=True, stop=True)
                        last.then_inc(su_done, 1)
                        for n in range(4):
                            nc.tensor.matmul(k.ps[:, a, n * P:(n + 1) * P], s[:, n // 2, n % 2, :], qd[:, 4 * a + n, :],
                                             start=True, stop=False)
                            last = nc.tensor.matmul(k.ps[:, a, n * P:(n + 1) * P], vn[:, n, :], qa[:, 4 * a + n, :],
                                                    start=False, stop=True)
                        last.then_inc(o_done, 1)
                        if beside:
                            project(of, tile + 1, 2, 9 * a + 6, 8 if a == 0 else 15)
                pe.wait_ge(osq_ready, g + 1)
                if not is_last:
                    pe.wait_ge(taken, g * DN_TILES + (DN_TILES + DN_CONVS))
                for v in range(2):
                    for b in range(2):
                        last = nc.tensor.matmul(k.ps[:, 2 + 2 * v + b, 0:TOK // 2], k.ones,
                                                sq[:, v, b * (TOK // 2):(b + 1) * (TOK // 2)], start=True, stop=True)
                last.then_inc(osum_done, 1)

            for i in range(DN_CONVS):
                if i >= 2:
                    pe.wait_ge(taken, i - 1)
                project(0, i, 2 * (i % 2), 0, 2 * KT - 1)
            with pe.Fori(0, DN_GROUPS - 1) as g:
                group(g, False)
            group(DN_GROUPS - 1, True)

        @block.scalar
        def _(act):
            def take(g, i, bank):
                act.wait_ge(tile_done, g * DN_TILES + (i + 1))
                ctx, lat = k.ps[:, bank, 0:CTX], k.ps[:, bank + 1, 0:LAT]
                if i < DN_CONVS:
                    nc.scalar.activation(raw[:, i, 2:2 + CTX], ctx, ACT.Copy)
                    nc.scalar.activation(raw[:, i, 2 + CTX + DN_GAP:2 + CTX + DN_GAP + LAT], lat, ACT.Copy).then_inc(taken, 1)
                else:
                    head = og[:, bass.ds(g * 2 + (i - DN_CONVS), 1), :].rearrange("p v t -> p (v t)")
                    nc.scalar.activation(head[:, 0:CTX], ctx, ACT.Silu)
                    nc.scalar.activation(head[:, CTX:TOK], lat, ACT.Silu).then_inc(taken, 1)

            def group(g, is_last):
                def feature(i):
                    act.wait_ge(conv_done, g * DN_CONVS + (i + 1))
                    dst = qk[:, i, :] if i < 2 else vf[:, i - 2, :]
                    nc.scalar.activation(dst, acc[:, i % 2, :], ACT.Silu).then_inc(featured, 1)

                feature(0)
                feature(1)
                act.wait_ge(on_ready, g)
                for i in range(2):
                    act.wait_ge(featured, g * DN_CONVS + (i + 1))
                    nc.scalar.activation(sq[:, i, :], qk[:, i, :], ACT.Square).then_inc(squared, 1)
                feature(2)
                feature(3)
                act.wait_ge(summed, g * 2 + 2)
                for i in range(2):
                    last = nc.scalar.activation(inv[:, i, :].rearrange("p (b n) -> p b n", b=2),
                                                k.ps[:, 4 + 2 * i:6 + 2 * i, 0:DN_CONV // 2], ACT.Ln, bias=k.eps)
                last.then_inc(log_ready, 1)
                act.wait_ge(log_ready, g + 1)
                nc.scalar.activation(inv, inv, ACT.Exp, scale=-0.5).then_inc(inv_ready, 1)
                for i in range(3):
                    act.wait_ge(turned, g * 3 + (i + 1))
                    dst = vtok[:, :, i, :] if i < 2 else ktok[:, :, :]
                    nc.scalar.activation(dst.rearrange("p (b c) d -> p b c d", b=2),
                                         k.ps[:, 2 * i:2 * i + 2, 0:3 * P].rearrange("p b (c d) -> p b c d", c=3),
                                         ACT.Copy).then_inc(tok_ready, 1)
                for pair in range(DN_PAIRS):
                    gp = g * DN_PAIRS + pair
                    beside = pair == 0 or not is_last
                    of, tile = (g, DN_CONVS) if pair == 0 else (g + 1, 2 * pair - 2)
                    act.wait_ge(diff_ready, gp + 1)
                    nc.scalar.activation(eg[:, :, :].rearrange("p n t -> p (n t)"),
                                         k.ps[:, 0:2, :].rearrange("p b n -> p (b n)"), ACT.Exp).then_inc(eg_ready, 1)
                    nc.scalar.activation(dec[:, :, :], dec[:, :, :], ACT.Exp).then_inc(dec_ready, 1)
                    act.wait_ge(xt_turned, gp + 1)
                    nc.scalar.activation(xx[:, :, 0, :], k.ps[:, 0:2, :].rearrange("p b (n t) -> p (b n) t", n=4),
                                         ACT.Copy).then_inc(x_ready, 1)
                    for level in range(1, LEVELS):
                        for a in range(2):
                            done = gp * (2 * (LEVELS - 1)) + 2 * (level - 1)
                            act.wait_ge(y_done, done + (a + 1))
                            nc.scalar.activation(y[:, 4 * a:4 * a + 4, :].rearrange("p n t -> p (n t)"), k.ps[:, a, :],
                                                 ACT.Copy).then_inc(y_ready, 1)
                    if beside:
                        take(of, tile, 6)
                    for a in range(2):
                        act.wait_ge(tr_done, gp * 2 + (a + 1))
                        for n in range(4):
                            d, v = n // 2, n % 2
                            ch = ORDERS[d][2 * pair + a]
                            last = nc.scalar.activation(vn[:, n, :], k.ps[:, 7, n * P:(n + 1) * P], ACT.Copy,
                                                        scale=gs[:, 3, d, ch, v:v + 1])
                        last.then_inc(vn_ready, 1)
                    if beside:
                        take(of, tile + 1, 2)
                act.wait_ge(o_ready, g * 6 + 6)
                nc.scalar.activation(sq[:, :, 0:TOK], o[:, :, :], ACT.Square).then_inc(osq_ready, 1)
                act.wait_ge(osum_done, g + 1)
                for v in range(2):
                    last = nc.scalar.activation(inv[:, v, 0:TOK].rearrange("p (b n) -> p b n", b=2),
                                                k.ps[:, 2 + 2 * v:4 + 2 * v, 0:TOK // 2], ACT.Ln, bias=k.eps, scale=1.0 / P)
                last.then_inc(olog_ready, 1)
                act.wait_ge(olog_ready, g + 1)
                nc.scalar.activation(inv[:, :, 0:TOK], inv[:, :, 0:TOK], ACT.Exp, scale=-0.5).then_inc(oinv_ready, 1)

            act.wait_ge(pad_ready, 1)
            for i in range(DN_CONVS):
                take(0, i, 2 * (i % 2))
            with act.Fori(0, DN_GROUPS - 1) as g:
                group(g, False)
            group(DN_GROUPS - 1, True)

        @block.gpsimd
        def _(pool):
            with pool.Fori(0, DN_GROUPS) as g:
                for pair in range(DN_PAIRS):
                    gp = g * DN_PAIRS + pair
                    pool.wait_ge(normed, g * 2 + 2)
                    pool.wait_ge(eg_ready, gp + 1)
                    if pair:
                        pool.wait_ge(o_done, g * 6 + 2 * pair)
                    for a in range(2):
                        for d in range(2):
                            ch, n = ORDERS[d][2 * pair + a], 4 * a + 2 * d
                            last = nc.gpsimd.tensor_tensor(
                                qd[:, n:n + 2, :], eg[:, n:n + 2, :],
                                qk[:, 0, conv_at(ch):conv_at(ch) + P].unsqueeze(1).broadcast_to([P, 2, P]), ALU.mult)
                    last.then_inc(qd_ready, 1)
                    pool.wait_ge(dec_ready, gp + 1)
                    pool.wait_ge(tok_ready, g * 3 + 3)
                    for n in range(8):
                        ch, d = chunk_of(pair, n), (n // 2) % 2
                        last = nc.gpsimd.tensor_tensor(kd[:, n, :], ktok[:, ch, :],
                                                       dec[:, n, last_of(d):last_of(d) + 1].broadcast_to([P, P]), ALU.mult)
                    last.then_inc(kd_ready, 1)

        @block.vector
        def _(dve):
            def convolve(g, i, j):
                wc = k.vec("dn_conv")[:, bass.ds(g * (DN_CONVS * DN_K) + (i * DN_K + j), 1)]
                if j == 0:
                    dve.wait_ge(taken, g * DN_TILES + (i + 1))
                    if i >= 2:
                        dve.wait_ge(featured, g * DN_CONVS + (i - 1))
                    nc.vector.tensor_scalar(acc[:, i % 2, :], raw[:, i, 0:DN_CONV], wc, None, ALU.mult).then_inc(tap, 1)
                else:
                    dve.wait_ge(tap, g * (DN_CONVS * (DN_K - 1)) + i * (DN_K - 1) + j)
                    nc.vector.scalar_tensor_tensor(acc[:, i % 2, :], raw[:, i, j:j + DN_CONV], wc, acc[:, i % 2, :],
                                                   ALU.mult, ALU.add).then_inc(tap if j < DN_K - 1 else conv_done, 1)

            def group(g, is_last):
                dve.wait_ge(og_ready, g)
                nc.vector.memset(s[:, :, :, :], 0.0).then_inc(state_zero, 1)
                nc.vector.tensor_copy(gs[:, :, :, :, :].rearrange("p q d c v -> p (q d c v)"),
                                      k.dn_gate[:, bass.ds(g, 1), :, :, :, :].rearrange("p g q d c v -> p (g q d c v)")
                                      ).then_inc(gs_ready, 1)
                for i in range(2, DN_CONVS):
                    for j in range(DN_K):
                        convolve(g, i, j)
                dve.wait_ge(inv_ready, g + 1)
                nc.vector.scalar_tensor_tensor(qk[:, 0, :], qk[:, 0, :], float(P) ** -0.5, inv[:, 0, :], ALU.mult,
                                               ALU.mult).then_inc(normed, 1)
                nc.vector.tensor_tensor(qk[:, 1, :], qk[:, 1, :], inv[:, 1, :], ALU.mult).then_inc(normed, 1)
                for ch in range(NC6):
                    dve.wait_ge(paired, g * NC6 + ((ch | 1) + 1))
                    nc.vector.tensor_tensor(
                        qkm[:, ch, :, :, :].rearrange("p d q t -> p d (q t)"),
                        k.ps[:, ch // 2, (ch % 2) * 2 * P:(ch % 2 + 1) * 2 * P].unsqueeze(1).broadcast_to([P, 2, 2 * P]),
                        k.keep, ALU.mult).then_inc(qkm_ready, 1)
                for pair in range(DN_PAIRS):
                    gp = g * DN_PAIRS + pair
                    if pair == 0:
                        dve.wait_ge(gs_ready, g + 1)
                        dve.wait_ge(qkm_ready, g * NC6 + NC6)
                    else:
                        dve.wait_ge(kd_ready, gp)
                    dve.wait_ge(gcb_ready, gp + 1)
                    for n in range(8):
                        ch, d, v = chunk_of(pair, n), (n // 2) % 2, n % 2
                        last = nc.vector.tensor_scalar(dec[:, n, :], k.ps[:, n // 4, (n % 4) * P:(n % 4 + 1) * P],
                                                       gs[:, 1, d, ch, v:v + 1], 0.0, ALU.subtract, ALU.min)
                    last.then_inc(diff_ready, 1)
                    dve.wait_ge(dec_ready, gp + 1)
                    for n in range(8):
                        ch, d, v = chunk_of(pair, n), (n // 2) % 2, n % 2
                        last = nc.vector.scalar_tensor_tensor(at[:, n, :], qkm[:, ch, d, 1, :], gs[:, 3, d, ch, v:v + 1],
                                                              dec[:, n, :], ALU.mult, ALU.mult)
                    last.then_inc(at_ready, 1)
                    if pair:
                        dve.wait_ge(o_done, g * 6 + 2 * pair)
                    for n in range(0, 8, 2):
                        ch, d = chunk_of(pair, n), (n // 2) % 2
                        last = nc.vector.tensor_tensor(qa[:, n:n + 2, :], dec[:, n:n + 2, :],
                                                       qkm[:, ch, d, 0, :].unsqueeze(1).broadcast_to([P, 2, P]), ALU.mult)
                    last.then_inc(qa_ready, 1)
                    dve.wait_ge(at_ready, gp + 1)
                    for level in range(LEVELS):
                        done = gp * (2 * (LEVELS - 1)) + 2 * (level - 1)
                        if level >= 2:
                            dve.wait_ge(y_done, done)
                        nc.vector.tensor_tensor(mt[:, :, :], at[:, :, :],
                                                k.beside[level].unsqueeze(1).broadcast_to([P, 8, P]), ALU.mult).then_inc(mt_ready, 1)
                        if level == 0:
                            dve.wait_ge(mt_ready, gp * LEVELS + 1)
                            if pair:
                                dve.wait_ge(tr_done, g * 6 + 2 * pair)
                            nc.vector.scalar_tensor_tensor(xx[:, :, 1, :], mt[:, :, :], -1.0,
                                                           k.ident.unsqueeze(1).broadcast_to([P, 8, P]),
                                                           ALU.mult, ALU.add).then_inc(xt_ready, 1)
                            dve.wait_ge(xt_ready, gp + 1)
                        if level >= 1:
                            if level == 1:
                                dve.wait_ge(x_ready, gp + 1)
                            for a in range(2):
                                step = 2 * (level - 1) + a
                                if pair == DN_PAIRS - 1 and not is_last and step < 2 * DN_K:
                                    convolve(g + 1, step // DN_K, step % DN_K)
                                dve.wait_ge(p_done, done + (a + 1))
                                if level >= 2:
                                    dve.wait_ge(xx_ready, done + (a - 1))
                                lo = 0 if level < LEVELS - 1 else 1
                                nc.vector.tensor_tensor(
                                    xx[:, 4 * a:4 * a + 4, lo:2, :].rearrange("p n x t -> p n (x t)"),
                                    xx[:, 4 * a:4 * a + 4, lo:2, :].rearrange("p n x t -> p n (x t)"),
                                    k.ps[:, 2 + 2 * a:4 + 2 * a, :].rearrange("p b (n x) -> p (b n) x", n=2)[:, :, lo * P:2 * P],
                                    ALU.subtract).then_inc(xx_ready, 1)
                    for a in range(2):
                        step = gp * 2 + a
                        dve.wait_ge(ks_done, step + 1)
                        for n in range(4):
                            d, v = n // 2, n % 2
                            ch = ORDERS[d][2 * pair + a]
                            last = nc.vector.scalar_tensor_tensor(r[:, n, :], k.ps[:, 6, n * P:(n + 1) * P], gs[:, 2, d, ch, v:v + 1],
                                                                  vtok[:, ch, v, :], ALU.mult, ALU.add)
                        last.then_inc(r_ready, 1)
                        dve.wait_ge(su_done, step + 1)
                        dve.wait_ge(o_done, step + 1)
                        dve.wait_ge(s_ready, step) if (pair or a) else dve.wait_ge(state_zero, g + 1)
                        for n in range(4):
                            d, v = n // 2, n % 2
                            last = nc.vector.scalar_tensor_tensor(s[:, d, v, :], s[:, d, v, :],
                                                                  eg[:, 4 * a + n, last_of(d):last_of(d) + 1],
                                                                  k.ps[:, 4 + a, n * P:(n + 1) * P], ALU.mult, ALU.add)
                        last.then_inc(s_ready, 1)
                        if pair or a:
                            dve.wait_ge(o_ready, step)
                        for d in range(2):
                            ch = ORDERS[d][2 * pair + a]
                            dst = o[:, :, ch * P:(ch + 1) * P]
                            src = k.ps[:, a, 2 * d * P:(2 * d + 2) * P].rearrange("p (v t) -> p v t", v=2)
                            if first_seen(d, ch):
                                last = nc.vector.tensor_copy(dst, src)
                            else:
                                last = nc.vector.tensor_tensor(dst, dst, src, ALU.add)
                        last.then_inc(o_ready, 1)
                dve.wait_ge(oinv_ready, g + 1)
                nc.vector.tensor_tensor(o[:, :, :], o[:, :, :], inv[:, :, 0:TOK], ALU.mult).then_inc(on_ready, 1)
                dve.wait_ge(on_ready, g + 1)
                dve.wait_ge(taken, g * DN_TILES + DN_TILES)
                heads = og[:, bass.ds(g * 2, 2), :].rearrange("p v t -> p (v t)")
                nc.vector.scalar_tensor_tensor(heads, o[:, :, :].rearrange("p v t -> p (v t)"), k.vec("dn_o_g"), heads,
                                               ALU.mult, ALU.mult).then_inc(og_ready, 1)

            nc.vector.memset(raw[:, :, :], 0.0).then_inc(pad_ready, 1)
            for i in range(2):
                for j in range(DN_K):
                    convolve(0, i, j)
            with dve.Fori(0, DN_GROUPS - 1) as g:
                group(g, False)
            group(DN_GROUPS - 1, True)
            dve.wait_ge(og_ready, DN_GROUPS)


def rotary(k, name, x, n_tiles, ntok, gain, swap, cos, sin):
    nc = k.nc
    r0 = ntok - LAT
    spans = spans_of(ntok)
    U = 2
    with ExitStack() as c:
        sem = lambda n: c.enter_context(nc.semaphore(f"{name}_{n}"))
        sb = lambda n, s: c.enter_context(nc.sbuf_tensor(f"{name}_{n}", s, FP32))
        xs, prod = sb("xs", [P, U, ntok]), sb("prod", [P, U, LAT])
        sq = inv = sb("sq", [P, U, ntok])
        fetched, squared, summed, log_ready, inv_ready = sem("fetched"), sem("squared"), sem("summed"), sem("log"), sem("inv")
        scaled, normed, swapped, prod_ready, cos_ready, out_ready = (sem(n) for n in "scaled normed swapped prod cos out".split())
        block = c.enter_context(nc.Block())
        tile = lambda t: x[:, bass.ds(t, 1), 0:ntok].rearrange("p a n -> p (a n)")

        @block.scalar
        def _(act):
            with act.Fori(0, n_tiles // U) as r:
                act.wait_ge(out_ready, r * U)
                for i in range(U):
                    nc.scalar.activation(xs[:, i, :], tile(r * U + i), ACT.Copy).then_inc(fetched, 1)
                if gain is not None:
                    for i in range(U):
                        act.wait_ge(fetched, r * U + (i + 1))
                        nc.scalar.activation(sq[:, i, :], xs[:, i, :], ACT.Square).then_inc(squared, 1)
                    for i in range(U):
                        act.wait_ge(summed, r * U + (i + 1))
                        for b, (t0, n) in enumerate(spans):
                            last = nc.scalar.activation(inv[:, i, t0:t0 + n], k.ps[:, 2 * i + b, 0:n], ACT.Ln, bias=k.eps,
                                                        scale=1.0 / P)
                        last.then_inc(log_ready, 1)
                    for i in range(U):
                        act.wait_ge(log_ready, r * U + (i + 1))
                        nc.scalar.activation(inv[:, i, :], inv[:, i, :], ACT.Exp, scale=-0.5).then_inc(inv_ready, 1)

        @block.tensor
        def _(pe):
            with pe.Fori(0, n_tiles // U) as r:
                if gain is not None:
                    for i in range(U):
                        pe.wait_ge(squared, r * U + (i + 1))
                        for b, (t0, n) in enumerate(spans):
                            last = nc.tensor.matmul(k.ps[:, 2 * i + b, 0:n], k.ones, sq[:, i, t0:t0 + n], start=True, stop=True)
                        last.then_inc(summed, 1)
                for i in range(U):
                    pe.wait_ge(normed if gain is not None else fetched, r * U + (i + 1))
                    nc.tensor.matmul(k.ps[:, 4 + i, :], swap, xs[:, i, r0:ntok], start=True, stop=True).then_inc(swapped, 1)

        @block.vector
        def _(dve):
            with dve.Fori(0, n_tiles // U) as r:
                if gain is not None:
                    for i in range(U):
                        dve.wait_ge(inv_ready, r * U + (i + 1))
                        nc.vector.scalar_tensor_tensor(xs[:, i, :], xs[:, i, :], gain, inv[:, i, :], ALU.mult,
                                                       ALU.mult).then_inc(normed, 1)
                for i in range(U):
                    if gain is not None:
                        dve.wait_ge(normed, r * U + (i + 1))
                        if r0:
                            nc.vector.tensor_copy(x[:, bass.ds(r * U + i, 1), 0:r0].rearrange("p a n -> p (a n)"), xs[:, i, 0:r0])
                    dve.wait_ge(swapped, r * U + (i + 1))
                    nc.vector.tensor_tensor(prod[:, i, :], k.ps[:, 4 + i, :], sin, ALU.mult).then_inc(prod_ready, 1)
                    nc.vector.tensor_tensor(xs[:, i, r0:ntok], xs[:, i, r0:ntok], cos, ALU.mult).then_inc(cos_ready, 1)
                for i in range(U):
                    dve.wait_ge(prod_ready, r * U + (i + 1))
                    dve.wait_ge(cos_ready, r * U + (i + 1))
                    nc.vector.tensor_tensor(x[:, bass.ds(r * U + i, 1), r0:ntok].rearrange("p a n -> p (a n)"), xs[:, i, r0:ntok],
                                            prod[:, i, :], ALU.add).then_inc(out_ready, 1)
            dve.wait_ge(out_ready, n_tiles)


def token_major(k, name, src, n_tiles, dst):
    nc = k.nc
    with ExitStack() as c:
        sem = lambda n: c.enter_context(nc.semaphore(f"{name}_{n}"))
        turned, taken = sem("turned"), sem("taken")
        block = c.enter_context(nc.Block())

        @block.tensor
        def _(pe):
            for t in range(n_tiles):
                if t >= 2:
                    pe.wait_ge(taken, t - 1)
                for ch in range(NC6):
                    last = nc.tensor.transpose(k.ps[:, 2 * (t % 2) + ch // 3, (ch % 3) * P:(ch % 3 + 1) * P],
                                               src(t, ch), k.ident)
                last.then_inc(turned, 1)

        @block.scalar
        def _(act):
            for t in range(n_tiles):
                act.wait_ge(turned, t + 1)
                nc.scalar.activation(dst[:, t, :, :].rearrange("p (b c) d -> p b c d", b=2),
                                     k.ps[:, 2 * (t % 2):2 * (t % 2) + 2, 0:3 * P].rearrange("p b (c d) -> p b c d", c=3),
                                     ACT.Copy).then_inc(taken, 1)
            act.wait_ge(taken, n_tiles)


def attend(k, name, q, kk, vtok, out, outer, inner, shared_kv, maps, scale, z=None, weights=None):
    nc = k.nc
    QT, HALF = LAT // P, TOK // 2
    units = QT * maps
    with ExitStack() as c:
        sem = lambda n: c.enter_context(nc.semaphore(f"{name}_{n}"))
        sb = lambda n, s: c.enter_context(nc.sbuf_tensor(f"{name}_{n}", s, FP32))
        qs, ks, vs = sb("qs", [P, LAT]), sb("ks", [P, TOK]), sb("vs", [P, NC6, P])
        prob = sb("prob", [P, 2, maps, TOK])
        pt = sb("pt", [P, NC6, LAT])
        mx, bias, total, recip, weight = (sb(n, [P, units]) for n in ("mx", "bias", "total", "recip", "weight"))
        fetched, scored, mx_ready, bias_ready, exp_ready, recip_ready, weight_ready, scaled, prob_ready = (
            sem(n) for n in "fetched scored mx bias exp recip weight scaled prob".split())
        turned, pt_ready, mixed, out_ready = (sem(n) for n in "turned pt mixed out".split())
        block = c.enter_context(nc.Block())

        def each(eng, body):
            for o in range(outer):
                with eng.Fori(0, inner) as j:
                    body(j + o * inner, o if shared_kv else j)

        def scores(par):
            return k.ps[:, 2 * par:2 * par + 2, 0:HALF]

        @block.tensor
        def _(pe):
            def body(h, kv):
                pe.wait_ge(fetched, h + 1)

                def score(u):
                    qt, m = u // maps, u % maps
                    rows = slice(64 * m, 64 * m + 64) if maps == 2 else slice(0, P)
                    if u >= 2:
                        pe.wait_ge(exp_ready, h * units + (u - 1))
                    for b in range(2):
                        last = nc.tensor.matmul(k.ps[:, 2 * (u % 2) + b, 0:HALF], qs[rows, qt * P:(qt + 1) * P],
                                                ks[rows, b * HALF:(b + 1) * HALF],
                                                start=True, stop=True)
                    last.then_inc(scored, 1)

                def turn(qt):
                    pe.wait_ge(prob_ready, h * QT + (qt + 1))
                    if qt:
                        pe.wait_ge(pt_ready, h * QT + qt)
                    for ch in range(NC6):
                        last = nc.tensor.transpose(k.ps[:, 4 + ch // 3, (ch % 3) * P:(ch % 3 + 1) * P],
                                                   prob[:, qt % 2, 0, ch * P:(ch + 1) * P], k.ident)
                    last.then_inc(turned, 1)

                for qt in range(QT):
                    for m in range(maps):
                        score(qt * maps + m)
                    if qt:
                        turn(qt - 1)
                turn(QT - 1)
                pe.wait_ge(pt_ready, h * QT + QT)
                pe.wait_ge(out_ready, h)
                for ch in range(NC6):
                    last = nc.tensor.matmul(k.ps[:, 6, :], vs[:, ch, :], pt[:, ch, :], start=(ch == 0), stop=(ch == NC6 - 1))
                last.then_inc(mixed, 1)
            each(pe, body)

        @block.scalar
        def _(act):
            def body(h, kv):
                act.wait_ge(mixed, h)
                nc.scalar.activation(qs[:, :], q[:, bass.ds(h, 1), :].rearrange("p a n -> p (a n)"), ACT.Copy)
                nc.scalar.activation(ks[:, :], kk[:, bass.ds(kv, 1), :].rearrange("p a n -> p (a n)"), ACT.Copy)
                v = vtok[:, bass.ds(kv, 1), :, :].rearrange("p a c d -> p (a c) d")
                nc.scalar.activation(vs[:, :, :], v, ACT.Copy).then_inc(fetched, 1)

                def take(qt):
                    act.wait_ge(turned, h * QT + (qt + 1))
                    nc.scalar.activation(pt[:, :, qt * P:(qt + 1) * P].rearrange("p (b c) d -> p b c d", b=2),
                                         k.ps[:, 4:6, 0:3 * P].rearrange("p b (c d) -> p b c d", c=3), ACT.Copy).then_inc(pt_ready, 1)

                for qt in range(QT):
                    for m in range(maps):
                        u = qt * maps + m
                        act.wait_ge(bias_ready, h * units + (u + 1))
                        if qt >= 2:
                            act.wait_ge(turned, h * QT + (qt - 1))
                        nc.scalar.activation(prob[:, qt % 2, m, :].rearrange("p (b n) -> p b n", b=2), scores(u % 2), ACT.Exp,
                                             bias=bias[:, u:u + 1], scale=scale, accum_out=total[:, u:u + 1]).then_inc(exp_ready, 1)
                    if qt:
                        take(qt - 1)
                take(QT - 1)
            each(act, body)

        @block.vector
        def _(dve):
            def body(h, kv):
                def bias_of(u):
                    dve.wait_ge(scored, h * units + (u + 1))
                    nc.vector.tensor_reduce(mx[:, u:u + 1], scores(u % 2), mybir.AxisListType.XY, ALU.max).then_inc(mx_ready, 1)
                    dve.wait_ge(mx_ready, h * units + (u + 1))
                    nc.vector.tensor_scalar(bias[:, u:u + 1], mx[:, u:u + 1], -scale, None, ALU.mult).then_inc(bias_ready, 1)

                def normalise(u):
                    qt, m = u // maps, u % maps
                    dve.wait_ge(exp_ready, h * units + (u + 1))
                    nc.vector.reciprocal(recip[:, u:u + 1], total[:, u:u + 1]).then_inc(recip_ready, 1)
                    dve.wait_ge(recip_ready, h * units + (u + 1))
                    if m:
                        nc.vector.tensor_scalar(weight[:, u:u + 1], recip[:, u:u + 1], weights, None, ALU.mult).then_inc(weight_ready, 1)
                        dve.wait_ge(weight_ready, h * QT + (qt + 1))
                        dve.wait_ge(scaled, h * QT + (qt + 1))
                        nc.vector.scalar_tensor_tensor(prob[:, qt % 2, 0, :], prob[:, qt % 2, 1, :], weight[:, u:u + 1],
                                                       prob[:, qt % 2, 0, :], ALU.mult, ALU.add).then_inc(prob_ready, 1)
                    else:
                        nc.vector.tensor_scalar(prob[:, qt % 2, 0, :], prob[:, qt % 2, 0, :], recip[:, u:u + 1], None,
                                                ALU.mult).then_inc(scaled if maps == 2 else prob_ready, 1)

                bias_of(0)
                for u in range(units):
                    if u + 1 < units:
                        bias_of(u + 1)
                    normalise(u)
                dve.wait_ge(mixed, h + 1)
                dst = out[:, bass.ds(h, 1), :].rearrange("p a n -> p (a n)")
                if z is None:
                    nc.vector.tensor_copy(dst, k.ps[:, 6, :]).then_inc(out_ready, 1)
                else:
                    nc.vector.tensor_tensor(dst, k.ps[:, 6, :], z[:, bass.ds(h, 1), :].rearrange("p a n -> p (a n)"),
                                            ALU.mult).then_inc(out_ready, 1)
            each(dve, body)
            dve.wait_ge(out_ready, outer * inner)


def take_tile(k, engine, dst, func=None):
    def take(t, s, banks):
        at = 0
        for b in banks:
            n = b.shape[-1]
            d = dst[:, bass.ds(t, 1), at:at + n].rearrange("p a n -> p (a n)")
            last = k.nc.scalar.activation(d, b, func or ACT.Copy) if engine == "scalar" else k.nc.vector.tensor_copy(d, b)
            at += n
        return last
    return take


def add_tile(k, h, gates):
    def take(t, s, banks):
        at = 0
        for b, (first, cond) in zip(banks, gates):
            n = b.shape[-1]
            d = h[:, bass.ds(t, 1), at:at + n].rearrange("p a n -> p (a n)")
            last = k.nc.vector.scalar_tensor_tensor(d, b, k.mod[:, bass.ds(t + first, 1), cond], d, ALU.mult, ALU.add)
            at += n
        return last
    return take


PAIRS = 4
PC = NC6 * 2
HW = 64
AUG = HW + 1
MRAW = TOK + 4
MLAT = CTX + 3


def mlstm_project(k, u, raw_q, raw_k, mv, mo):
    nc = k.nc
    lat = [(CTX, LAT)]
    src = lambda kt, t0, n: u[:, kt, t0:t0 + n]
    tile = lambda a, t, lo, n: a[:, bass.ds(t, 1), lo:lo + n].rearrange("p a n -> p (a n)")

    def take_q(t, s, banks):
        return nc.vector.tensor_copy(tile(raw_q, t, 1, LAT), banks[0])

    def take_k(t, s, banks):
        nc.vector.tensor_copy(tile(raw_k, t, 1, CTX), banks[0])
        return nc.vector.tensor_copy(tile(raw_k, t, MLAT, LAT), banks[1])

    linear(k, "mq", k.io["l0_w_mq"], src, KT, PAIRS, lat, take_q, unroll=4)
    linear(k, "mk", k.io["l0_w_mk"], src, KT, PAIRS, spans_of(TOK), take_k)
    linear(k, "mv", k.io["l0_w_mv"], src, KT, PAIRS, spans_of(TOK), take_tile(k, "vector", mv))
    linear(k, "mo", k.io["l0_w_mo"], src, KT, PAIRS, lat, take_tile(k, "scalar", mo, ACT.Sigmoid), unroll=4, on="scalar")


def mlstm_convolve(k, raw_q, raw_k, q, kk):
    nc = k.nc
    with ExitStack() as c:
        sem = lambda n: c.enter_context(nc.semaphore(f"mc_{n}"))
        acc = c.enter_context(nc.sbuf_tensor("mc_acc", [P, 2 * PAIRS, MRAW - 2], FP32))
        tap, conv_done, q_ready, scaled, k_ready = sem("tap"), sem("conv"), sem("q"), sem("scaled"), sem("k")
        padded = sem("padded")
        block = c.enter_context(nc.Block())

        @block.vector
        def _(dve):
            nc.vector.memset(raw_q[:, :, 0:1], 0.0)
            nc.vector.memset(raw_q[:, :, LAT + 1:LAT + 2], 0.0)
            nc.vector.memset(raw_k[:, :, 0:1], 0.0)
            nc.vector.memset(raw_k[:, :, 1 + CTX:MLAT], 0.0)
            nc.vector.memset(raw_k[:, :, MRAW - 1:MRAW], 0.0).then_inc(padded, 1)
            dve.wait_ge(padded, 1)
            for j in range(3):
                if j:
                    dve.wait_ge(tap, j)
                for t in range(2 * PAIRS):
                    raw, n = (raw_q[:, t, :], LAT) if t < PAIRS else (raw_k[:, t - PAIRS, :], MRAW - 2)
                    w = k.vec("m_conv")[:, t * 3 + j:t * 3 + j + 1]
                    if j == 0:
                        last = nc.vector.tensor_scalar(acc[:, t, 0:n], raw[:, 0:n], w, None, ALU.mult)
                    else:
                        last = nc.vector.scalar_tensor_tensor(acc[:, t, 0:n], raw[:, j:j + n], w, acc[:, t, 0:n], ALU.mult, ALU.add)
                last.then_inc(tap if j < 2 else conv_done, 1)
            dve.wait_ge(q_ready, 1)
            nc.vector.tensor_scalar(q[:, :, :], q[:, :, :], float(HW) ** -0.5, None, ALU.mult).then_inc(scaled, 1)
            dve.wait_ge(scaled, 1)

        @block.scalar
        def _(act):
            act.wait_ge(conv_done, 1)
            nc.scalar.activation(q[:, :, :], acc[:, 0:PAIRS, 0:LAT], ACT.Silu).then_inc(q_ready, 1)
            nc.scalar.activation(kk[:, :, 0:CTX], acc[:, PAIRS:2 * PAIRS, 0:CTX], ACT.Silu)
            nc.scalar.activation(kk[:, :, CTX:TOK], acc[:, PAIRS:2 * PAIRS, MLAT - 1:MLAT - 1 + LAT], ACT.Silu).then_inc(k_ready, 1)
            act.wait_ge(k_ready, 1)


def mlstm_gates(k, u):
    nc = k.nc
    W = PAIRS * PC
    names = "inp fg mag lf b a cm0 cm1 cmt bl am mp nn tmp".split()
    with ExitStack() as c:
        sem = lambda n: c.enter_context(nc.semaphore(f"mg_{n}"))
        t = namedtuple("Steps", names)(*[c.enter_context(nc.sbuf_tensor(f"mg_{n}", [P, 2, HW], FP32)) for n in names])
        w = c.enter_context(nc.sbuf_tensor("mg_w", [P, KT, 32], FP32))
        amc = c.enter_context(nc.sbuf_tensor("mg_amc", [P, 1], FP32))
        diag = c.enter_context(nc.sbuf_tensor("mg_diag", [P, P], FP32))
        (w_ready, projected, zeroed, pre_ready, mag_ready, exp_ready, log_ready, lf_ready, summed, a_ready, turned, cm_step,
         am_ready, diag_ready, back, cmt_ready, m_step, n_ready, arg_ready, out_ready, dec_ready) = (sem(n) for n in (
            "w projected zeroed pre mag exp log lf summed a turned cm am diag back cmt m n arg out dec").split())
        block = c.enter_context(nc.Block())
        o = k.mg
        cols = lambda a, d: a[:, d, 0:W]
        by = lambda a, d: a[:, d, 0:W].rearrange("p (r c i) -> p r c i", r=PAIRS, i=2)
        at_chunk = lambda a, d, ch: by(a, d)[:, :, ch, :]
        flat = lambda a: a[:, :, :].rearrange("p d n -> p (d n)")
        shifts = [1, 2, 4, 8, 16, 32, 64]

        @block.sync
        def _(sp):
            sp.dma_start(w[:, :, :].rearrange("p a b -> p (a b)"), k.io["l0_w_mg"]).then_inc(w_ready, 16)

        @block.tensor
        def _(pe):
            pe.wait_ge(w_ready, 16)
            for ch in range(NC6):
                for kt in range(KT):
                    last = nc.tensor.matmul(k.ps[:, 0, ch * 32:(ch + 1) * 32], u[:, kt, ch * P:(ch + 1) * P], w[:, kt, :],
                                            start=(kt == 0), stop=(kt == KT - 1))
            last.then_inc(projected, 1)
            pe.wait_ge(lf_ready, 1)
            for d in range(2):
                nc.tensor.matmul(k.ps[:, 1, d * HW:(d + 1) * HW], k.tri[d], t.lf[:, d, :], start=True, stop=True)
            nc.tensor.matmul(k.ps[:, 1, P:2 * P], k.ones, flat(t.lf), start=True, stop=True).then_inc(summed, 1)
            pe.wait_ge(a_ready, 1)
            nc.tensor.transpose(k.ps[:, 2, 0:P], flat(t.a), k.ident).then_inc(turned, 1)
            pe.wait_ge(diag_ready, 1)
            last_cm = (t.cm0, t.cm1)[len(shifts) % 2]
            nc.tensor.transpose(k.ps[:, 3, 0:P], flat(last_cm), k.ident)
            nc.tensor.matmul(k.ps[:, 3, P:2 * P], k.ones, diag[:, :], start=True, stop=True).then_inc(back, 1)

        @block.vector
        def _(dve):
            nc.vector.memset(flat(t.fg), 40.0)
            for a in (t.inp, t.mp, t.nn):
                last = nc.vector.memset(flat(a), 0.0)
            last.then_inc(zeroed, 1)
            dve.wait_ge(zeroed, 1)
            dve.wait_ge(projected, 1)
            pre = k.ps[:, 0, 0:NC6 * 32].rearrange("p (c q r i) -> p q r c i", c=NC6, q=4, i=2)
            bias = k.vec("m_gate_b").rearrange("p (q r i) -> p q r i", q=4, i=2)
            for d in range(2):
                for q, dst in ((2 * d, t.inp), (2 * d + 1, t.fg)):
                    last = nc.vector.tensor_tensor(by(dst, d), pre[:, q, :, :, :],
                                                   bias[:, q, :, :].unsqueeze(2).broadcast_to([P, PAIRS, NC6, 2]), ALU.add)
            last.then_inc(pre_ready, 1)
            dve.wait_ge(pre_ready, 1)
            nc.vector.scalar_tensor_tensor(flat(t.mag), flat(t.fg), -1.0, flat(t.fg), ALU.mult, ALU.max).then_inc(mag_ready, 1)
            dve.wait_ge(log_ready, 1)
            nc.vector.scalar_tensor_tensor(flat(t.lf), flat(t.fg), 0.0, flat(t.mag), ALU.min, ALU.subtract).then_inc(lf_ready, 1)
            dve.wait_ge(summed, 1)
            nc.vector.tensor_copy(flat(t.b), k.ps[:, 1, 0:P])
            nc.vector.tensor_copy(flat(t.bl), k.ps[:, 1, P:2 * P])
            nc.vector.tensor_tensor(flat(t.a), flat(t.inp), k.ps[:, 1, 0:P], ALU.subtract).then_inc(a_ready, 1)
            dve.wait_ge(turned, 1)
            nc.vector.tensor_copy(flat(t.cm0), k.ps[:, 2, 0:P]).then_inc(cm_step, 1)
            for i, sh in enumerate(shifts):
                src, dst = flat((t.cm0, t.cm1)[i % 2]), flat((t.cm1, t.cm0)[i % 2])
                dve.wait_ge(cm_step, i + 1)
                nc.vector.tensor_copy(dst[0:HW, 0:sh], src[0:HW, 0:sh])
                nc.vector.tensor_tensor(dst[0:HW, sh:P], src[0:HW, sh:P], src[0:HW, 0:P - sh], ALU.max)
                nc.vector.tensor_copy(dst[HW:P, P - sh:P], src[HW:P, P - sh:P])
                nc.vector.tensor_tensor(dst[HW:P, 0:P - sh], src[HW:P, 0:P - sh], src[HW:P, sh:P], ALU.max).then_inc(cm_step, 1)
            dve.wait_ge(cm_step, len(shifts) + 1)
            cm = flat((t.cm0, t.cm1)[len(shifts) % 2])
            nc.vector.tensor_copy(amc[0:HW, :], cm[0:HW, P - 1:P])
            nc.vector.tensor_copy(amc[HW:P, :], cm[HW:P, 0:1]).then_inc(am_ready, 1)
            dve.wait_ge(am_ready, 1)
            nc.vector.tensor_scalar(diag[:, :], k.ident, amc[:, :], None, ALU.mult).then_inc(diag_ready, 1)
            dve.wait_ge(back, 1)
            nc.vector.tensor_copy(flat(t.cmt), k.ps[:, 3, 0:P])
            nc.vector.tensor_copy(flat(t.am), k.ps[:, 3, P:2 * P]).then_inc(cmt_ready, 1)
            dve.wait_ge(cmt_ready, 1)
            for j in range(NC6):
                for d in range(2):
                    ch = ORDERS[d][j]
                    last = nc.vector.tensor_tensor(at_chunk(t.nn, d, ch), at_chunk(t.mp, d, ch), at_chunk(t.am, d, ch), ALU.max)
                last.then_inc(m_step, 1)
                dve.wait_ge(m_step, 2 * j + 1)
                if j + 1 < NC6:
                    for d in range(2):
                        ch, after = ORDERS[d][j], ORDERS[d][j + 1]
                        last = nc.vector.tensor_tensor(at_chunk(t.mp, d, after), at_chunk(t.nn, d, ch), at_chunk(t.bl, d, ch), ALU.add)
                    last.then_inc(m_step, 1)
                    dve.wait_ge(m_step, 2 * j + 2)
            nc.vector.tensor_tensor(flat(o.n), flat(t.mp), flat(t.cmt), ALU.max).then_inc(n_ready, 1)
            dve.wait_ge(n_ready, 1)
            nc.vector.tensor_copy(flat(o.a), flat(t.a))
            nc.vector.tensor_tensor(flat(o.inter), flat(t.mp), flat(o.n), ALU.subtract)
            nc.vector.tensor_tensor(flat(o.ws), flat(t.a), flat(t.nn), ALU.subtract)
            nc.vector.tensor_tensor(flat(t.am), flat(t.mp), flat(t.nn), ALU.subtract)
            nc.vector.scalar_tensor_tensor(flat(t.tmp), flat(t.b), -1.0, flat(o.n), ALU.mult, ALU.subtract).then_inc(arg_ready, 1)
            dve.wait_ge(arg_ready, 1)
            nc.vector.tensor_scalar(flat(o.floor), flat(t.tmp), 80.0, None, ALU.min).then_inc(arg_ready, 1)
            dve.wait_ge(out_ready, 1)
            for i in range(2):
                rows_ = slice(i * HW, (i + 1) * HW)
                for d in range(2):
                    last = nc.vector.tensor_copy(o.decay[rows_, d, :, :], by(t.am, d)[rows_, :, :, i])
            last.then_inc(dec_ready, 1)
            dve.wait_ge(dec_ready, 1)

        @block.scalar
        def _(act):
            act.wait_ge(mag_ready, 1)
            nc.scalar.activation(flat(t.mag), flat(t.mag), ACT.Exp, scale=-1.0).then_inc(exp_ready, 1)
            act.wait_ge(exp_ready, 1)
            nc.scalar.activation(flat(t.mag), flat(t.mag), ACT.Ln, bias=1.0).then_inc(log_ready, 1)
            act.wait_ge(arg_ready, 2)
            nc.scalar.activation(flat(o.inter), flat(o.inter), ACT.Exp)
            nc.scalar.activation(flat(o.ws), flat(o.ws), ACT.Exp)
            nc.scalar.activation(flat(o.floor), flat(o.floor), ACT.Exp)
            nc.scalar.activation(flat(t.am), flat(t.am), ACT.Exp).then_inc(out_ready, 1)


def mlstm_turn(k, kk, mv, ktok, vaug):
    nc = k.nc
    with ExitStack() as c:
        turned = c.enter_context(nc.semaphore("mt_turned"))
        taken = c.enter_context(nc.semaphore("mt_taken"))
        ones_ready = c.enter_context(nc.semaphore("mt_ones"))
        block = c.enter_context(nc.Block())

        @block.tensor
        def _(pe):
            for t in range(2 * PAIRS):
                if t >= 2:
                    pe.wait_ge(taken, t - 1)
                for ch in range(NC6):
                    src = (kk if t < PAIRS else mv)[:, t % PAIRS, ch * P:(ch + 1) * P]
                    last = nc.tensor.transpose(k.ps[:, 2 * (t % 2) + ch // 3, (ch % 3) * P:(ch % 3 + 1) * P], src, k.ident)
                last.then_inc(turned, 1)

        @block.vector
        def _(dve):
            nc.vector.memset(vaug[:, :, :, HW:AUG], 1.0).then_inc(ones_ready, 1)
            dve.wait_ge(ones_ready, 1)

        @block.scalar
        def _(act):
            for t in range(2 * PAIRS):
                act.wait_ge(turned, t + 1)
                for b in range(2):
                    src = k.ps[:, 2 * (t % 2) + b, 0:3 * P]
                    if t < PAIRS:
                        last = nc.scalar.activation(ktok[:, t, b * 3 * P:(b + 1) * 3 * P], src, ACT.Copy)
                    else:
                        last = nc.scalar.activation(vaug[:, t - PAIRS, 6 * b:6 * b + 6, 0:HW],
                                                    src.rearrange("p (c d) -> p c d", d=HW), ACT.Copy)
                last.then_inc(taken, 1)
            act.wait_ge(taken, 2 * PAIRS)


def mlstm_mix(k, q, kk, ktok, vaug, hsum):
    nc = k.nc
    LC = LAT // P
    g_ = k.mg
    with ExitStack() as c:
        sem = lambda n: c.enter_context(nc.semaphore(f"mm_{n}"))
        sb = lambda n, s: c.enter_context(nc.sbuf_tensor(f"mm_{n}", s, FP32))
        qs, ks = sb("qs", [P, LAT]), sb("ks", [P, LAT])
        st = sb("st", [P, 2, LC * 2, P])
        e = sb("e", [P, 2, LC * 2, P])
        ns = sb("ns", [P, 2, PC])
        kw = sb("kw", [P, 2, NC6, P])
        va = sb("va", [P, NC6, 2 * AUG])
        state = sb("state", [P, 2, 2 * AUG])
        fresh = sb("fresh", [P, 2, 2 * AUG])
        num = sb("num", [P, 4, AUG])
        den = sb("den", [P, 4])
        neg = sb("neg", [P, 4])
        (fetched, vec_fetched, paired, kqm_ready, nb_done, diff_ready, e_ready, st_ready, kw_ready, zeroed, qc_done, up_done,
         fresh_ready, state_ready, part_ready, num_ready, neg_ready, abs_ready, den_ready, recip_ready, h_ready) = (sem(n) for n in (
            "fetched vec_fetched paired kqm nb diff e st kw zeroed qc up fresh state part num neg abs den recip h").split())
        block = c.enter_context(nc.Block())

        @block.scalar
        def _(act):
            with act.Fori(0, PAIRS) as g:
                act.wait_ge(h_ready, g * LC)
                act.wait_ge(state_ready, g * NC6)
                nc.scalar.activation(qs[:, :], q[:, bass.ds(g, 1), :].rearrange("p a n -> p (a n)"), ACT.Copy)
                nc.scalar.activation(ks[:, :], kk[:, bass.ds(g, 1), CTX:TOK].rearrange("p a n -> p (a n)"), ACT.Copy)
                nc.scalar.activation(va[:, :, :].rearrange("p c n -> p (c n)"),
                                     vaug[:, bass.ds(g, 1), :, :].rearrange("p a c n -> p (a c n)"), ACT.Copy).then_inc(fetched, 1)
                act.wait_ge(diff_ready, g + 1)
                nc.scalar.activation(e[:, :, :, :], e[:, :, :, :], ACT.Exp, scale=-1.0).then_inc(e_ready, 1)

        @block.tensor
        def _(pe):
            with pe.Fori(0, PAIRS) as g:
                pe.wait_ge(fetched, g + 1)
                pe.wait_ge(vec_fetched, g + 1)
                for i8 in range(2 * LC):
                    i, ch = i8 // LC, i8 % LC
                    rows_ = slice(i * HW, (i + 1) * HW)
                    last = nc.tensor.matmul(k.ps[:, i8 // 4, (i8 % 4) * P:(i8 % 4 + 1) * P], ks[rows_, ch * P:(ch + 1) * P],
                                            qs[rows_, ch * P:(ch + 1) * P], start=True, stop=True)
                last.then_inc(paired, 1)
                for d in range(2):
                    for i8 in range(2 * LC):
                        col = 2 * (i8 % LC + 2) + i8 // LC
                        last = nc.tensor.matmul(k.ps[:, 2 + 2 * d + i8 // 4, (i8 % 4) * P:(i8 % 4 + 1) * P],
                                                ns[:, d, col:col + 1].broadcast_to([P, P]), k.ident, start=True, stop=True)
                last.then_inc(nb_done, 1)
                pe.wait_ge(kw_ready, g + 1)
                pe.wait_ge(kqm_ready, g + 1)
                pe.wait_ge(zeroed, g + 1)
                for j in range(NC6):
                    if j >= 2:
                        pe.wait_ge(fresh_ready, g * NC6 + (j - 1))
                    for d in range(2):
                        last = nc.tensor.matmul(k.ps[:, j % 2, d * 2 * AUG:(d + 1) * 2 * AUG], kw[:, d, ORDERS[d][j], :],
                                                va[:, ORDERS[d][j], :], start=True, stop=True)
                    last.then_inc(up_done, 1)
                    if j >= 2:
                        if j == 2:
                            pe.wait_ge(st_ready, g + 1)
                        else:
                            pe.wait_ge(part_ready, g * LC + j - 2)
                        pe.wait_ge(state_ready, g * NC6 + j)
                        for d in range(2):
                            ch = ORDERS[d][j]
                            nc.tensor.matmul(k.ps[:, 6, d * 2 * AUG:(d + 1) * 2 * AUG], qs[:, (ch - 2) * P:(ch - 1) * P],
                                             state[:, d, :], start=True, stop=True)
                            for i in range(2):
                                last = nc.tensor.matmul(k.ps[:, 7, (2 * d + i) * AUG:(2 * d + i + 1) * AUG],
                                                        st[:, d, i * LC + ch - 2, :], va[:, ch, i * AUG:(i + 1) * AUG],
                                                        start=True, stop=True)
                        last.then_inc(qc_done, 1)

        @block.vector
        def _(dve):
            with dve.Fori(0, PAIRS) as g:
                dve.wait_ge(nb_done, g)
                nc.vector.tensor_copy(ns[:, :, :], g_.n[:, :, bass.ds(g * PC, PC)]).then_inc(vec_fetched, 1)
                for d in range(2):
                    last = nc.vector.tensor_tensor(
                        kw[:, d, :, :].rearrange("p c (i f) -> p (c i) f", i=2),
                        ktok[:, bass.ds(g, 1), :].rearrange("p a (n f) -> p (a n) f", f=HW),
                        g_.ws[:, d, bass.ds(g * PC, PC)].unsqueeze(2).broadcast_to([P, PC, HW]), ALU.mult)
                last.then_inc(kw_ready, 1)
                nc.vector.memset(state[:, :, :], 0.0).then_inc(zeroed, 1)
                dve.wait_ge(nb_done, g + 1)
                for d in range(2):
                    for i8 in range(2 * LC):
                        col = 2 * (i8 % LC + 2) + i8 // LC
                        last = nc.vector.tensor_scalar(e[:, d, i8, :], k.ps[:, 2 + 2 * d + i8 // 4, (i8 % 4) * P:(i8 % 4 + 1) * P],
                                                       g_.a[:, d, bass.ds(g * PC + col, 1)], 0.0, ALU.subtract, ALU.max)
                last.then_inc(diff_ready, 1)
                dve.wait_ge(paired, g + 1)
                for d in range(2):
                    last = nc.vector.tensor_tensor(st[:, d, :, :], k.ps[:, 0:2, :].rearrange("p b (n t) -> p (b n) t", t=P),
                                                   k.tri[d].unsqueeze(1).broadcast_to([P, 2 * LC, P]), ALU.mult)
                last.then_inc(kqm_ready, 1)
                dve.wait_ge(kqm_ready, g + 1)
                dve.wait_ge(e_ready, g + 1)
                nc.vector.tensor_tensor(st[:, :, :, :], st[:, :, :, :], e[:, :, :, :], ALU.mult).then_inc(st_ready, 1)
                for j in range(NC6):
                    dve.wait_ge(up_done, g * NC6 + j + 1)
                    dve.wait_ge(state_ready, g * NC6 + j)
                    nc.vector.tensor_tensor(fresh[:, :, :], k.ps[:, j % 2, 0:4 * AUG].rearrange("p (d n) -> p d n", d=2),
                                            k.con("halves").unsqueeze(1).broadcast_to([P, 2, 2 * AUG]), ALU.mult).then_inc(fresh_ready, 1)
                    if j >= 2:
                        dve.wait_ge(qc_done, g * LC + j - 1)
                        dve.wait_ge(h_ready, g * LC + j - 2)
                        for d in range(2):
                            ch = ORDERS[d][j]
                            for i in range(2):
                                n = 2 * d + i
                                col = 2 * ch + i
                                last = nc.vector.tensor_scalar(num[:, n, :], k.ps[:, 6, n * AUG:(n + 1) * AUG],
                                                               g_.inter[:, d, bass.ds(g * PC + col, 1)], None, ALU.mult)
                        last.then_inc(num_ready, 1)
                    dve.wait_ge(fresh_ready, g * NC6 + j + 1)
                    dve.wait_ge(zeroed, g + 1) if j == 0 else dve.wait_ge(state_ready, g * NC6 + j)
                    for d in range(2):
                        last = nc.vector.scalar_tensor_tensor(state[:, d, :], state[:, d, :],
                                                              g_.decay[:, d, bass.ds(g, 1), ORDERS[d][j]], fresh[:, d, :],
                                                              ALU.mult, ALU.add)
                    last.then_inc(state_ready, 1)
                    if j >= 2:
                        s4 = g * LC + j - 1
                        dve.wait_ge(num_ready, 2 * s4 - 1)
                        nc.vector.tensor_tensor(num[:, :, :].rearrange("p n f -> p (n f)"), num[:, :, :].rearrange("p n f -> p (n f)"),
                                                k.ps[:, 7, 0:4 * AUG], ALU.add).then_inc(num_ready, 1)
                        dve.wait_ge(num_ready, 2 * s4)
                        nc.vector.tensor_scalar(neg[:, :], num[:, :, HW], -1.0, None, ALU.mult).then_inc(part_ready, 1)
                        dve.wait_ge(part_ready, s4)
                        nc.vector.tensor_tensor(den[:, :], neg[:, :], num[:, :, HW], ALU.max).then_inc(abs_ready, 1)
                        dve.wait_ge(abs_ready, s4)
                        for d in range(2):
                            last = nc.vector.tensor_tensor(den[:, 2 * d:2 * d + 2], den[:, 2 * d:2 * d + 2],
                                                           g_.floor[:, d, bass.ds(g * PC + 2 * ORDERS[d][j], 2)], ALU.max)
                        last.then_inc(den_ready, 1)
                        dve.wait_ge(den_ready, s4)
                        nc.vector.reciprocal(neg[:, :], den[:, :]).then_inc(recip_ready, 1)
                        dve.wait_ge(recip_ready, s4)
                        for d in range(2):
                            ch = ORDERS[d][j]
                            if j > 2:
                                dve.wait_ge(h_ready, s4 - 1)
                            for i in range(2):
                                n = 2 * d + i
                                dst = hsum[:, ch - 2, bass.ds(g * 2 + i, 1), :].rearrange("p a f -> p (a f)")
                                if first_seen(d, ch):
                                    last = nc.vector.tensor_scalar(dst, num[:, n, 0:HW], neg[:, n:n + 1], None, ALU.mult)
                                else:
                                    last = nc.vector.scalar_tensor_tensor(dst, num[:, n, 0:HW], neg[:, n:n + 1], dst, ALU.mult, ALU.add)
                        last.then_inc(h_ready, 1)
            dve.wait_ge(h_ready, PAIRS * LC)


def mlstm_finish(k, hsum, mo, mix):
    nc = k.nc
    LC, H = LAT // P, 2 * PAIRS
    with ExitStack() as c:
        sem = lambda n: c.enter_context(nc.semaphore(f"mf_{n}"))
        sq = c.enter_context(nc.sbuf_tensor("mf_sq", [P, LC * H, HW], FP32))
        ss = c.enter_context(nc.sbuf_tensor("mf_ss", [P, LC * H], FP32))
        squared, summed, log_ready, inv_ready, normed, turned, taken = (sem(n) for n in "squared summed log inv normed turned taken".split())
        block = c.enter_context(nc.Block())
        hs = hsum[:, :, :, :].rearrange("p c h f -> p (c h) f")

        @block.scalar
        def _(act):
            nc.scalar.activation(sq[:, :, :], hs, ACT.Square).then_inc(squared, 1)
            act.wait_ge(summed, 1)
            nc.scalar.activation(ss[:, :], ss[:, :], ACT.Ln, bias=k.eps, scale=1.0 / HW).then_inc(log_ready, 1)
            act.wait_ge(log_ready, 1)
            nc.scalar.activation(ss[:, :], ss[:, :], ACT.Exp, scale=-0.5).then_inc(inv_ready, 1)

        @block.vector
        def _(dve):
            dve.wait_ge(squared, 1)
            nc.vector.reduce_sum(ss[:, :], sq[:, :, :], AX).then_inc(summed, 1)
            dve.wait_ge(inv_ready, 1)
            nc.vector.tensor_tensor(hs, hs, ss[:, :].unsqueeze(2).broadcast_to([P, LC * H, HW]), ALU.mult).then_inc(normed, 1)
            for t in range(PAIRS):
                dve.wait_ge(turned, t + 1)
                nc.vector.scalar_tensor_tensor(mix[:, t, :], k.ps[:, t, :], k.vec("m_norm_g")[:, t:t + 1], mo[:, t, :],
                                               ALU.mult, ALU.mult).then_inc(taken, 1)
            dve.wait_ge(taken, PAIRS)

        @block.tensor
        def _(pe):
            pe.wait_ge(normed, 1)
            for t in range(PAIRS):
                for ch in range(LC):
                    last = nc.tensor.transpose(k.ps[:, t, ch * P:(ch + 1) * P],
                                               hsum[:, ch, 2 * t:2 * t + 2, :].rearrange("p h f -> p (h f)"), k.ident)
                last.then_inc(turned, 1)


def diff_weight(k, weight):
    nc = k.nc
    with ExitStack() as c:
        sem = lambda n: c.enter_context(nc.semaphore(f"dw_{n}"))
        prod = c.enter_context(nc.sbuf_tensor("dw_prod", [P, 2, HW], FP32))
        dots = c.enter_context(nc.sbuf_tensor("dw_dots", [P, 2], FP32))
        prod_ready, dots_ready, exp_ready, out_ready = sem("prod"), sem("dots"), sem("exp"), sem("out")
        block = c.enter_context(nc.Block())

        @block.vector
        def _(dve):
            lam = k.vec("lambdas").rearrange("p (s n) -> p s n", s=4)
            nc.vector.tensor_tensor(prod[:, :, :], lam[:, 0:2, :], lam[:, 2:4, :], ALU.mult).then_inc(prod_ready, 1)
            dve.wait_ge(prod_ready, 1)
            nc.vector.reduce_sum(dots[:, :], prod[:, :, :], AX).then_inc(dots_ready, 1)
            dve.wait_ge(exp_ready, 1)
            nc.vector.scalar_tensor_tensor(weight[:, :], dots[:, 1:2], -LAM_INIT, dots[:, 0:1], ALU.add,
                                           ALU.subtract).then_inc(out_ready, 1)
            dve.wait_ge(out_ready, 1)

        @block.scalar
        def _(act):
            act.wait_ge(dots_ready, 1)
            nc.scalar.activation(dots[:, :], dots[:, :], ACT.Exp).then_inc(exp_ready, 1)


LAM_INIT = 0.8 - 0.6


def head_norm(k, name, x, n_tiles, dst, gain, ln_scale):
    nc = k.nc
    with ExitStack() as c:
        sem = lambda n: c.enter_context(nc.semaphore(f"{name}_{n}"))
        sq = c.enter_context(nc.sbuf_tensor(f"{name}_sq", [P, n_tiles, LAT], FP32))
        squared, summed, log_ready, inv_ready, out_ready = (sem(n) for n in "squared summed log inv out".split())
        block = c.enter_context(nc.Block())

        @block.scalar
        def _(act):
            for t in range(n_tiles):
                nc.scalar.activation(sq[:, t, :], x[:, t, :], ACT.Square).then_inc(squared, 1)
            act.wait_ge(summed, 1)
            nc.scalar.activation(sq[:, :, :], k.ps[:, 0:n_tiles, :], ACT.Ln, bias=k.eps, scale=1.0 / P).then_inc(log_ready, 1)
            act.wait_ge(log_ready, 1)
            nc.scalar.activation(sq[:, :, :], sq[:, :, :], ACT.Exp, scale=-0.5, bias=ln_scale).then_inc(inv_ready, 1)

        @block.tensor
        def _(pe):
            for t in range(n_tiles):
                pe.wait_ge(squared, t + 1)
                last = nc.tensor.matmul(k.ps[:, t, :], k.ones, sq[:, t, :], start=True, stop=True)
            last.then_inc(summed, 1)

        @block.vector
        def _(dve):
            dve.wait_ge(inv_ready, 1)
            for t in range(n_tiles):
                last = nc.vector.scalar_tensor_tensor(dst[:, t, :], x[:, t, :], gain[:, t:t + 1], sq[:, t, :], ALU.mult, ALU.mult)
            last.then_inc(out_ready, 1)
            dve.wait_ge(out_ready, 1)


def take_x(k, h, x, gain):
    nc = k.nc
    with ExitStack() as c:
        taken = c.enter_context(nc.semaphore("x_taken"))
        block = c.enter_context(nc.Block())

        @block.vector
        def _(dve):
            nc.vector.tensor_copy(x[:, :, :], h[:, :, CTX:TOK]).then_inc(taken, 1)
            dve.wait_ge(taken, 1)
    if gain is not None:
        norm_residual(k, "final", None, x, gain, None)


FT = 22
EXPERTS = 8
CONV_W = 31


def gated_up(k, name, w, src, n_pairs, take_first, take_second, then=None):
    nc = k.nc
    U = 2
    with ExitStack() as c:
        sem = lambda n: c.enter_context(nc.semaphore(f"{name}_{n}"))
        ring = c.enter_context(nc.sbuf_tensor(f"{name}_ring", [P, U, 2, D], FP32))
        act_out = c.enter_context(nc.sbuf_tensor(f"{name}_act", [P, U, LAT], FP32))
        w_ready = [sem(f"w_ready{s}") for s in range(U)]
        pair_done, first_taken, taken = sem("pair_done"), sem("first_taken"), sem("taken")
        block = c.enter_context(nc.Block())
        rounds = n_pairs // U

        @block.sync
        def _(sp):
            for s in range(U):
                sp.dma_start(ring[:, s, :, :], w[s]).then_inc(w_ready[s], 16)
            with sp.Fori(1, rounds) as r:
                for s in range(U):
                    sp.wait_ge(pair_done, r * U + (s + 1 - U))
                    sp.dma_start(ring[:, s, :, :], w[r * U + s]).then_inc(w_ready[s], 16)

        @block.tensor
        def _(pe):
            with pe.Fori(0, rounds) as r:
                for s in range(U):
                    pe.wait_ge(w_ready[s], r * 16 + 16)
                    pe.wait_ge(taken, r * U)
                    for half in range(2):
                        for kt in range(KT):
                            last = nc.tensor.matmul(k.ps[:, 2 * s + half, :], ring[:, s, half, kt * P:(kt + 1) * P], src(kt),
                                                    start=(kt == 0), stop=(kt == KT - 1))
                    last.then_inc(pair_done, 1)

        @block.scalar
        def _(act):
            with act.Fori(0, rounds) as r:
                for s in range(U):
                    act.wait_ge(pair_done, r * U + (s + 1))
                    act.wait_ge(taken, r * U)
                    take_first(r * U + s, act_out[:, s, :], k.ps[:, 2 * s, :]).then_inc(first_taken, 1)

        @block.vector
        def _(dve):
            with dve.Fori(0, rounds) as r:
                for s in range(U):
                    dve.wait_ge(first_taken, r * U + (s + 1))
                    take_second(r * U + s, act_out[:, s, :], k.ps[:, 2 * s + 1, :]).then_inc(taken, 1)
                if then is not None:
                    dve.wait_ge(taken, r * U + U)
                    then(dve, r)
            dve.wait_ge(taken, n_pairs)


def depthwise(k, padded, y, tap):
    nc = k.nc

    def convolve(dve, r):
        for j in range(CONV_W):
            for i in range(2):
                if j:
                    dve.wait_ge(tap[i], r * CONV_W + j)
                out = y[:, bass.ds(r * 2 + i, 1), :].rearrange("p a n -> p (a n)")
                src = padded[:, bass.ds(r * 2 + i, 1), j:j + LAT].rearrange("p a n -> p (a n)")
                w = k.vec("dw_taps")[:, bass.ds(r * (2 * CONV_W) + (i * CONV_W + j), 1)]
                if j == 0:
                    nc.vector.tensor_scalar(out, src, w, k.vec("l1_conv_dw_b")[:, bass.ds(r * 2 + i, 1)], ALU.mult,
                                            ALU.add).then_inc(tap[i], 1)
                else:
                    nc.vector.scalar_tensor_tensor(out, src, w, out, ALU.mult, ALU.add).then_inc(tap[i], 1)
    return convolve


def layer_norm_silu(k, y):
    nc = k.nc
    with ExitStack() as c:
        sem = lambda n: c.enter_context(nc.semaphore(f"ln_{n}"))
        sq = c.enter_context(nc.sbuf_tensor("ln_sq", [P, KT, LAT], FP32))
        mean = c.enter_context(nc.sbuf_tensor("ln_mean", [P, LAT], FP32))
        inv = c.enter_context(nc.sbuf_tensor("ln_inv", [P, LAT], FP32))
        summed, mean_ready, centred, squared, var_done, log_ready, inv_ready, scaled, out_ready = (
            sem(n) for n in "summed mean centred squared var log inv scaled out".split())
        block = c.enter_context(nc.Block())

        @block.tensor
        def _(pe):
            for kt in range(KT):
                last = nc.tensor.matmul(k.ps[:, 0, :], k.ones, y[:, kt, :], start=(kt == 0), stop=(kt == KT - 1))
            last.then_inc(summed, 1)
            for kt in range(KT):
                pe.wait_ge(squared, kt + 1)
                last = nc.tensor.matmul(k.ps[:, 1, :], k.ones, sq[:, kt, :], start=(kt == 0), stop=(kt == KT - 1))
            last.then_inc(var_done, 1)

        @block.scalar
        def _(act):
            act.wait_ge(summed, 1)
            nc.scalar.activation(mean[:, :], k.ps[:, 0, :], ACT.Copy, scale=1.0 / D).then_inc(mean_ready, 1)
            for kt in range(KT):
                act.wait_ge(centred, kt + 1)
                nc.scalar.activation(sq[:, kt, :], y[:, kt, :], ACT.Square).then_inc(squared, 1)
            act.wait_ge(var_done, 1)
            nc.scalar.activation(inv[:, :], k.ps[:, 1, :], ACT.Ln, bias=k.eps, scale=1.0 / D).then_inc(log_ready, 1)
            act.wait_ge(log_ready, 1)
            nc.scalar.activation(inv[:, :], inv[:, :], ACT.Exp, scale=-0.5).then_inc(inv_ready, 1)
            for kt in range(KT):
                act.wait_ge(scaled, kt + 1)
                nc.scalar.activation(y[:, kt, :], y[:, kt, :], ACT.Silu, scale=k.vec("l1_conv_ln_g")[:, kt:kt + 1],
                                     bias=k.vec("l1_conv_ln_b")[:, kt:kt + 1]).then_inc(out_ready, 1)
            act.wait_ge(out_ready, KT)

        @block.vector
        def _(dve):
            dve.wait_ge(mean_ready, 1)
            for kt in range(KT):
                nc.vector.tensor_tensor(y[:, kt, :], y[:, kt, :], mean[:, :], ALU.subtract).then_inc(centred, 1)
            dve.wait_ge(inv_ready, 1)
            dve.wait_ge(centred, KT)
            for kt in range(KT):
                nc.vector.tensor_tensor(y[:, kt, :], y[:, kt, :], inv[:, :], ALU.mult).then_inc(scaled, 1)


def second_block(k, x):
    nc = k.nc
    mod = lambda first, cond: k.mod[:, first:first + KT, cond]
    sb = lambda c, n, s: c.enter_context(nc.sbuf_tensor(n, s, FP32))
    with ExitStack() as c:
        mix = sb(c, "mix", [P, KT, LAT])
        u = k.u
        with ExitStack() as c1:
            xc = sb(c1, "xc", [P, KT, TOK])
            with_context(k, x, xc)
            norm_modulate(k, "n2", xc, u, TOK, k.vec("l0_mix_pre_g"),
                          [(0, CTX, mod(56, 3), mod(48, 3)), (CTX, LAT, mod(56, 2), mod(48, 2))])
        with ExitStack() as c1:
            wide = ("n", "a", "inter", "ws", "floor")
            k.mg = namedtuple("Gates", wide + ("decay",))(*[sb(c1, "m_" + n, [P, 2, HW]) for n in wide],
                                                          sb(c1, "m_decay", [P, 2, PAIRS, NC6]))
            mo, q, kk = sb(c1, "m_o", [P, PAIRS, LAT]), sb(c1, "m_q", [P, PAIRS, LAT]), sb(c1, "m_k", [P, PAIRS, TOK])
            ktok, vaug = sb(c1, "m_ktok", [P, PAIRS, TOK]), sb(c1, "m_vaug", [P, PAIRS, PC, AUG])
            mlstm_gates(k, u)
            recycle(k)
            with ExitStack() as c2:
                mv = sb(c2, "m_v", [P, PAIRS, TOK])
                with ExitStack() as c3:
                    raw_q, raw_k = sb(c3, "m_raw_q", [P, PAIRS, LAT + 2]), sb(c3, "m_raw_k", [P, PAIRS, MRAW])
                    mlstm_project(k, u, raw_q, raw_k, mv, mo)
                    mlstm_convolve(k, raw_q, raw_k, q, kk)
                mlstm_turn(k, kk, mv, ktok, vaug)
            hsum = sb(c1, "m_hsum", [P, LAT // P, 2 * PAIRS, HW])
            mlstm_mix(k, q, kk, ktok, vaug, hsum)
            mlstm_finish(k, hsum, mo, mix)
        recycle(k)
        with ExitStack() as c1:
            dq, dk, vtok = sb(c1, "d_q", [P, 4, LAT]), sb(c1, "d_k", [P, 4, TOK]), sb(c1, "d_vtok", [P, 4, NC6, P])
            weight, od = sb(c1, "d_weight", [P, 1]), sb(c1, "d_o", [P, 4, LAT])
            src = lambda kt, t0, n: u[:, kt, t0:t0 + n]
            diff_weight(k, weight)
            linear(k, "dq", k.io["l0_w_dq"], src, KT, 4, [(CTX, LAT)], take_tile(k, "vector", dq), unroll=4)
            linear(k, "dk", k.io["l0_w_dk"], src, KT, 4, spans_of(TOK), take_tile(k, "vector", dk))
            tables = sb(c1, "rope_2_sb", [P, 2 * LAT + P])
            load(k, "rope_tables_2", tables[:, :], "rope_2")
            rope = (tables[:, 2 * LAT:2 * LAT + P], tables[:, 0:LAT], tables[:, LAT:2 * LAT])
            rotary(k, "rq2", dq, 4, LAT, None, *rope)
            rotary(k, "rk2", dk, 4, TOK, None, *rope)
            with nc.sbuf_tensor("d_v", [P, 4, TOK], FP32) as dv:
                linear(k, "dv", k.io["l0_w_dv"], src, KT, 4, spans_of(TOK), take_tile(k, "vector", dv))
                token_major(k, "diff_v", lambda t, ch: dv[:, t, ch * P:(ch + 1) * P], 4, vtok)
            attend(k, "diff", dq, dk, vtok, od, 1, 4, False, 2, float(HW) ** -0.5, weights=weight[:, :])
            head_norm(k, "dn2", od, 4, mix[:, 4:8, :], k.vec("diff_norm_g"), k.con("ln_rest"))
        y = u[:, :, 0:LAT]
        linear(k, "l0_out", k.io["l0_w_out"], lambda kt, t0, n: mix[:, kt, :], KT, KT, [(0, LAT)], take_tile(k, "vector", y), unroll=4)
        norm_residual(k, "r0", x, y, k.vec("l0_mix_post_g"), mod(64, 2))
    recycle(k)
    with ExitStack() as c:
        u, hidden, y = k.u[:, :, 0:LAT], sb(c, "hidden", [P, FT, LAT]), sb(c, "y3", [P, KT, LAT])
        norm_modulate(k, "n3", x, u, LAT, k.vec("l0_ffn_pre_g"), [(0, LAT, mod(80, 2), mod(72, 2))])
        gated_up(k, "ffn", k.io["ffn_up"], lambda kt: u[:, kt, :], FT,
                 lambda t, tmp, ps: nc.scalar.activation(tmp, ps, ACT.Silu),
                 lambda t, tmp, ps: nc.vector.tensor_tensor(hidden[:, bass.ds(t, 1), :].rearrange("p a n -> p (a n)"), tmp, ps, ALU.mult))
        linear(k, "ffn_d", k.io["ffn_down"], lambda kt, t0, n: hidden[:, kt, :], FT, KT, [(0, LAT)], take_tile(k, "vector", y), unroll=4)
        norm_residual(k, "r1", x, y, k.vec("l0_ffn_post_g"), mod(88, 2))
    with ExitStack() as c:
        u, padded, y = k.u[:, :, 0:LAT], sb(c, "padded", [P, KT, LAT + CONV_W - 1]), sb(c, "y4", [P, KT, LAT])
        norm_modulate(k, "n4", x, u, LAT, k.vec("l1_mix_pre_g"), [(0, LAT, mod(104, 2), mod(96, 2))])
        zero_edges(k, padded)
        edge = CONV_W // 2
        bias = k.vec("l1_conv_pw1_b")
        gated_up(k, "pw1", k.io["pw1"], lambda kt: u[:, kt, :], KT,
                 lambda t, tmp, ps: nc.scalar.activation(tmp, ps, ACT.Sigmoid, bias=bias[:, bass.ds(t + KT, 1)]),
                 lambda t, tmp, ps: nc.vector.scalar_tensor_tensor(
                     padded[:, bass.ds(t, 1), edge:edge + LAT].rearrange("p a n -> p (a n)"), ps, bias[:, bass.ds(t, 1)], tmp,
                     ALU.add, ALU.mult),
                 then=depthwise(k, padded, y, [c.enter_context(nc.semaphore(f"dwc_tap{i}")) for i in range(2)]))
        layer_norm_silu(k, y)
        linear(k, "pw2", k.io["pw2"], lambda kt, t0, n: y[:, kt, :], KT, KT, [(0, LAT)],
               lambda t, s, banks: nc.vector.tensor_scalar(u[:, bass.ds(t, 1), :].rearrange("p a n -> p (a n)"), banks[0],
                                                           k.vec("l1_conv_pw2_b")[:, bass.ds(t, 1)], None, ALU.add), unroll=4)
        norm_residual(k, "r2", x, u, k.vec("l1_mix_post_g"), mod(112, 2))
    recycle(k)
    with ExitStack() as c:
        u, y = k.u[:, :, 0:LAT], sb(c, "y5", [P, KT, LAT])
        norm_modulate(k, "n5", x, u, LAT, k.vec("l1_ffn_pre_g"), [(0, LAT, mod(128, 2), mod(120, 2))])
        experts(k, u, y)
        norm_residual(k, "r3", x, y, k.vec("l1_ffn_post_g"), mod(136, 2))


def zero_edges(k, padded):
    nc = k.nc
    edge = CONV_W // 2
    with ExitStack() as c:
        zeroed = c.enter_context(nc.semaphore("edges_zeroed"))
        block = c.enter_context(nc.Block())

        @block.vector
        def _(dve):
            nc.vector.memset(padded[:, :, 0:edge], 0.0)
            nc.vector.memset(padded[:, :, edge + LAT:LAT + 2 * edge], 0.0).then_inc(zeroed, 1)
            dve.wait_ge(zeroed, 1)


def with_context(k, x, xc):
    nc = k.nc
    with ExitStack() as c:
        loaded = c.enter_context(nc.semaphore("ctx2_loaded"))
        taken = c.enter_context(nc.semaphore("ctx2_taken"))
        block = c.enter_context(nc.Block())

        @block.sync
        def _(sp):
            sp.dma_start(xc[:, :, 0:CTX], k.io["ctx_2"]).then_inc(loaded, 16)
            sp.wait_ge(loaded, 16)

        @block.vector
        def _(dve):
            nc.vector.tensor_copy(xc[:, :, CTX:TOK], x[:, :, :]).then_inc(taken, 1)
            dve.wait_ge(taken, 1)


SLOTS = P
BLOCKS = (2 * LAT - EXPERTS) // SLOTS + EXPERTS
CHUNKS = 12
WIDE = 10
FAR = 1e30


def chunk_tiles(c):
    return 2 if c < WIDE else 1


def route(k, u, r):
    nc = k.nc
    TT = LAT // P
    with ExitStack() as c:
        sem = lambda n: c.enter_context(nc.semaphore(f"rt_{n}"))
        sb = lambda n, s, t=FP32: c.enter_context(nc.sbuf_tensor(f"rt_{n}", s, t))
        w = sb("w", [P, KT, EXPERTS])
        logits, best = sb("logits", [P, TT, EXPERTS]), sb("best", [P, 2, TT, EXPERTS])
        at = sb("at", [P, 2, TT, EXPERTS], U32)
        atf, gap = sb("atf", [P, 2, TT]), sb("gap", [P, TT])
        pick, chosen = sb("pick", [P, 2, TT, EXPERTS]), sb("chosen", [P, TT, EXPERTS])
        rank, count = sb("rank", [P, TT, EXPERTS]), sb("count", [P, EXPERTS])
        ends, eb = sb("ends", [P, EXPERTS + 1]), sb("eb", [P, BLOCKS])
        (w_ready, projected, logits_ready, max_ready, at_ready, atf_ready, pick_ready, masked, gap_ready, gate_ready, chosen_ready,
         ranked, rank_ready, n_ready, end_ready, slot_step, slot_ready, expert_step, expert_ready) = (
            sem(n) for n in "w projected logits max at atf pick masked gap gate chosen ranked rank n end sstep slot estep expert".split())
        block = c.enter_context(nc.Block())

        @block.sync
        def _(sp):
            sp.dma_start(w[:, :, :].rearrange("p a b -> p (a b)"), k.io["router"]).then_inc(w_ready, 16)

        @block.tensor
        def _(pe):
            pe.wait_ge(w_ready, 16)
            for t in range(TT):
                for kt in range(KT):
                    last = nc.tensor.matmul(k.ps[:, 0, t * EXPERTS:(t + 1) * EXPERTS], u[:, kt, t * P:(t + 1) * P], w[:, kt, :],
                                            start=(kt == 0), stop=(kt == KT - 1))
            last.then_inc(projected, 1)
            pe.wait_ge(chosen_ready, 1)
            before = k.keep[:, 0, P:2 * P]
            for t in range(TT):
                out = k.ps[:, 1, t * EXPERTS:(t + 1) * EXPERTS]
                nc.tensor.matmul(out, before, chosen[:, t, :], start=True, stop=(t == 0))
                for t2 in range(t):
                    nc.tensor.matmul(out, k.ones, chosen[:, t2, :], start=False, stop=(t2 == t - 1))
            for t in range(TT):
                last = nc.tensor.matmul(k.ps[:, 1, TT * EXPERTS:(TT + 1) * EXPERTS], k.ones, chosen[:, t, :],
                                        start=(t == 0), stop=(t == TT - 1))
            last.then_inc(ranked, 1)

        @block.vector
        def _(dve):
            names = k.con("experts").unsqueeze(1).broadcast_to([P, TT, EXPERTS])
            wide = lambda a: a.unsqueeze(2).broadcast_to([P, TT, EXPERTS])
            dve.wait_ge(projected, 1)
            nc.vector.tensor_copy(logits[:, :, :].rearrange("p t e -> p (t e)"), k.ps[:, 0, 0:TT * EXPERTS]).then_inc(logits_ready, 1)
            for n in range(2):
                dve.wait_ge(logits_ready, n + 1)
                for t in range(TT):
                    last = nc.vector.max(best[:, n, t, :], logits[:, t, :])
                last.then_inc(max_ready, 1)
                dve.wait_ge(max_ready, n + 1)
                for t in range(TT):
                    last = nc.vector.max_index(at[:, n, t, :], best[:, n, t, :], logits[:, t, :])
                last.then_inc(at_ready, 1)
                dve.wait_ge(at_ready, n + 1)
                nc.vector.tensor_copy(atf[:, n, :], at[:, n, :, 0]).then_inc(atf_ready, 1)
                dve.wait_ge(atf_ready, n + 1)
                nc.vector.tensor_tensor(pick[:, n, :, :], wide(atf[:, n, :]), names, ALU.is_equal).then_inc(pick_ready, 1)
                dve.wait_ge(pick_ready, n + 1)
                if n == 0:
                    nc.vector.scalar_tensor_tensor(logits[:, :, :], pick[:, 0, :, :], -FAR, logits[:, :, :], ALU.mult,
                                                   ALU.add).then_inc(logits_ready, 1)
            nc.vector.tensor_tensor(gap[:, :], best[:, 0, :, 0], best[:, 1, :, 0], ALU.subtract).then_inc(gap_ready, 1)
            nc.vector.tensor_tensor(chosen[:, :, :], pick[:, 0, :, :], pick[:, 1, :, :], ALU.add).then_inc(chosen_ready, 1)
            nc.vector.memset(ends[:, 0:1], 0.0)
            nc.vector.memset(ends[:, 1:EXPERTS + 1], 0.0)
            nc.vector.memset(eb[:, :], 0.0).then_inc(n_ready, 1)
            dve.wait_ge(ranked, 1)
            nc.vector.tensor_copy(rank[:, :, :].rearrange("p t e -> p (t e)"), k.ps[:, 1, 0:TT * EXPERTS])
            nc.vector.tensor_copy(count[:, :], k.ps[:, 1, TT * EXPERTS:(TT + 1) * EXPERTS]).then_inc(rank_ready, 1)
            dve.wait_ge(rank_ready, 1)
            for j in range(LAT // SLOTS):
                dve.wait_ge(n_ready, j + 1)
                nc.vector.scalar_tensor_tensor(ends[:, 1:EXPERTS + 1], count[:, :], float(j * SLOTS), ends[:, 1:EXPERTS + 1],
                                               ALU.is_gt, ALU.add).then_inc(n_ready, 1)
            dve.wait_ge(n_ready, LAT // SLOTS + 1)
            for e in range(1, EXPERTS):
                if e > 1:
                    dve.wait_ge(end_ready, e - 1)
                nc.vector.tensor_tensor(ends[:, e + 1:e + 2], ends[:, e + 1:e + 2], ends[:, e:e + 1], ALU.add).then_inc(end_ready, 1)
            dve.wait_ge(end_ready, EXPERTS - 1)
            nc.vector.scalar_tensor_tensor(rank[:, :, :], ends[:, 0:EXPERTS].unsqueeze(1).broadcast_to([P, TT, EXPERTS]),
                                           float(SLOTS), rank[:, :, :], ALU.mult, ALU.add).then_inc(slot_step, 1)
            dve.wait_ge(slot_step, 1)
            for n in range(2):
                last = nc.vector.tensor_tensor(pick[:, n, :, :], pick[:, n, :, :], rank[:, :, :], ALU.mult)
            last.then_inc(slot_step, 1)
            dve.wait_ge(slot_step, 2)
            nc.vector.reduce_sum(r.slot[:, :, :].rearrange("p n t -> p (n t)"), pick[:, :, :, :].rearrange("p n t e -> p (n t) e"),
                                 AX).then_inc(slot_ready, 1)
            for e in range(EXPERTS):
                if e:
                    dve.wait_ge(expert_step, e)
                nc.vector.scalar_tensor_tensor(eb[:, :], k.con("numbers")[:, 0:BLOCKS], ends[:, e + 1:e + 2], eb[:, :],
                                               ALU.is_ge, ALU.add).then_inc(expert_step, 1)
            dve.wait_ge(expert_step, EXPERTS)
            nc.vector.tensor_scalar(eb[:, :], eb[:, :], float(EXPERTS - 1), None, ALU.min).then_inc(expert_step, 1)
            dve.wait_ge(expert_step, EXPERTS + 1)
            nc.vector.tensor_copy(r.expert[:, :], eb[:, :])
            nc.vector.tensor_copy(r.used[:, :], ends[:, EXPERTS:EXPERTS + 1]).then_inc(expert_ready, 1)
            dve.wait_ge(expert_ready, 1)
            dve.wait_ge(slot_ready, 1)

        @block.scalar
        def _(act):
            act.wait_ge(gap_ready, 1)
            nc.scalar.activation(r.gate[:, 0, :], gap[:, :], ACT.Sigmoid)
            nc.scalar.activation(r.gate[:, 1, :], gap[:, :], ACT.Sigmoid, scale=-1.0).then_inc(gate_ready, 1)
            act.wait_ge(gate_ready, 1)


def turn_tokens(k, u, utok):
    nc = k.nc
    TT = LAT // P
    with ExitStack() as c:
        turned, taken = c.enter_context(nc.semaphore("ut_turned")), c.enter_context(nc.semaphore("ut_taken"))
        block = c.enter_context(nc.Block())

        @block.tensor
        def _(pe):
            for t in range(TT):
                for kt in range(KT):
                    last = nc.tensor.transpose(k.ps[:, 2 * t + kt // 4, (kt % 4) * P:(kt % 4 + 1) * P], u[:, kt, t * P:(t + 1) * P],
                                               k.ident)
                last.then_inc(turned, 1)

        @block.scalar
        def _(act):
            for t in range(TT):
                act.wait_ge(turned, t + 1)
                nc.scalar.activation(utok[:, t, :].rearrange("p (b n) -> p b n", b=2), k.ps[:, 2 * t:2 * t + 2, :],
                                     ACT.Copy).then_inc(taken, 1)
            act.wait_ge(taken, TT)


def experts(k, u, y):
    nc = k.nc
    TT, UR, DR = LAT // P, 3, 4
    with ExitStack() as c:
        sem = lambda n: c.enter_context(nc.semaphore(f"moe_{n}"))
        sb = lambda n, s, t=FP32: c.enter_context(nc.sbuf_tensor(f"moe_{n}", s, t))
        r = namedtuple("Routes", "slot gate expert used")(sb("slot", [P, 2, TT]), sb("gate", [P, 2, TT]), sb("expert", [P, BLOCKS], U32),
                                                         sb("used", [P, 1], U32))
        utok = sb("utok", [P, TT, D])
        route(k, u, r)
        turn_tokens(k, u, utok)
        up_ring, down_ring = sb("up_ring", [P, UR, KT * 4 * P]), sb("down_ring", [P, DR, 2 * D])
        hot = sb("hot", [P, TT, SLOTS])
        gated = sb("gated", [P, TT, SLOTS])
        second = sb("second", [P, TT, SLOTS])
        spread = sb("spread", [P, LAT])
        xg = sb("xg", [P, KT, SLOTS])
        act_out, hidden = sb("act", [P, 2, 2 * P]), sb("hidden", [P, 2, 2 * P])
        ht = sb("ht", [P, 2, 2 * P])
        yb = sb("yb", [P, D])
        up_ready = [sem(f"up_ready{s}") for s in range(UR)]
        down_ready = [sem(f"down_ready{s}") for s in range(DR)]
        (zeroed, hot1, hot_ready, gated1, gated_ready, moved, gathered, xg_ready, gates_turned, spread_ready, up_done, silu_ready,
         h_ready, h_turned, ht_ready, down_done, down_last, yb_ready, combined, summed, finished) = (
            sem(n) for n in ("zeroed hot1 hot gated1 gated moved gathered xg gates_turned spread up_done silu h h_turned ht "
                             "down_done down_last yb combined summed finished").split())
        block = c.enter_context(nc.Block())
        up_wide, up_narrow, down_wide, down_narrow = (k.io[n] for n in ("moe_up", "moe_up_narrow", "moe_down", "moe_down_narrow"))
        n_wide, n_narrow = WIDE, CHUNKS - WIDE

        def blocks_used(eng):
            return eng.value_load(r.used[0:1, 0:1], min_val=2 * LAT // SLOTS, max_val=BLOCKS)

        @block.sync
        def _(sp):
            def stream(b):
                e = sp.value_load(r.expert[0:1, bass.ds(b, 1)], min_val=0, max_val=EXPERTS - 1)
                for ch in range(CHUNKS):
                    n = chunk_tiles(ch)
                    up, down = ((up_wide[e * n_wide + ch], down_wide[e * n_wide + ch]) if ch < WIDE else
                                (up_narrow[e * n_narrow + (ch - WIDE)], down_narrow[e * n_narrow + (ch - WIDE)]))
                    if not isinstance(b, int) or ch >= UR:
                        sp.wait_ge(up_done, b * CHUNKS + (ch - UR + 1))
                    sp.dma_start(up_ring[:, ch % UR, 0:n * 2 * D], up).then_inc(up_ready[ch % UR], 16)
                    if not isinstance(b, int) or ch >= DR:
                        sp.wait_ge(down_done, b * CHUNKS + (ch - DR + 1))
                    sp.dma_start(down_ring[:, ch % DR, 0:n * D], down).then_inc(down_ready[ch % DR], 16)
            stream(0)
            used = blocks_used(sp)
            with sp.Fori(1, BLOCKS) as b:
                with sp.If(b < used):
                    stream(b)

        @block.tensor
        def _(pe):
            used = blocks_used(pe)
            with pe.Fori(0, BLOCKS) as b:
                with pe.If(b < used):
                    pe.wait_ge(hot_ready, b + 1)
                    pe.wait_ge(summed, b * KT)
                    for dt in range(KT):
                        for t in range(TT):
                            last = nc.tensor.matmul(k.ps[:, 6 + dt // 4, (dt % 4) * P:(dt % 4 + 1) * P], utok[:, t, dt * P:(dt + 1) * P],
                                                    hot[:, t, :], start=(t == 0), stop=(t == TT - 1))
                    last.then_inc(gathered, 1)
                    pe.wait_ge(gated_ready, b + 1)
                    pe.wait_ge(ht_ready, b * CHUNKS)
                    for t in range(TT):
                        last = nc.tensor.transpose(k.ps[:, 3, t * P:(t + 1) * P], gated[:, t, :], k.ident)
                    last.then_inc(gates_turned, 1)
                    pe.wait_ge(xg_ready, b + 1)
                    pe.wait_ge(yb_ready, b)

                    def up(ch):
                        w = chunk_tiles(ch) * 2 * P
                        pe.wait_ge(up_ready[ch % UR], b * (16 * CHUNKS // UR) + 16 * (ch // UR + 1))
                        if ch >= 2:
                            pe.wait_ge(h_ready, b * CHUNKS + (ch - 1))
                        else:
                            pe.wait_ge(h_ready, b * CHUNKS)
                        for kt in range(KT):
                            last = nc.tensor.matmul(k.ps[:, ch % 2, 0:w], xg[:, kt, :], up_ring[:, ch % UR, kt * w:(kt + 1) * w],
                                                    start=(kt == 0), stop=(kt == KT - 1))
                        last.then_inc(up_done, 1)

                    def turn(ch):
                        pe.wait_ge(h_ready, b * CHUNKS + (ch + 1))
                        if ch == 1:
                            pe.wait_ge(spread_ready, b + 1)
                        if ch >= 2:
                            pe.wait_ge(ht_ready, b * CHUNKS + (ch - 1))
                        for f in range(chunk_tiles(ch)):
                            last = nc.tensor.transpose(k.ps[:, 2 + ch % 2, f * P:(f + 1) * P], hidden[:, ch % 2, f * P:(f + 1) * P], k.ident)
                        last.then_inc(h_turned, 1)

                    def down(ch):
                        pe.wait_ge(ht_ready, b * CHUNKS + (ch + 1))
                        pe.wait_ge(down_ready[ch % DR], b * (16 * CHUNKS // DR) + 16 * (ch // DR + 1))
                        for f in range(chunk_tiles(ch)):
                            for half in range(2):
                                last = nc.tensor.matmul(k.ps[:, 4 + half, :], ht[:, ch % 2, f * P:(f + 1) * P],
                                                        down_ring[:, ch % DR, f * D + half * BANK:f * D + (half + 1) * BANK],
                                                        start=(ch == 0 and f == 0), stop=(ch == CHUNKS - 1 and f == chunk_tiles(ch) - 1))
                        last.then_inc(down_done, 1)

                    for ch in range(CHUNKS + 2):
                        if ch < CHUNKS:
                            up(ch)
                        if 1 <= ch <= CHUNKS:
                            turn(ch - 1)
                        if ch >= 2:
                            down(ch - 2)
                    pe.wait_ge(yb_ready, b + 1)
                    for dt in range(KT):
                        if dt >= 2:
                            pe.wait_ge(summed, b * KT + (dt - 1))
                        nc.tensor.matmul(k.ps[:, 6 + dt % 2, :], yb[:, dt * P:(dt + 1) * P], spread[:, :], start=True,
                                         stop=True).then_inc(combined, 1)

        @block.scalar
        def _(act):
            used = blocks_used(act)
            with act.Fori(0, BLOCKS) as b:
                with act.If(b < used):
                    act.wait_ge(gathered, b + 1)
                    nc.scalar.activation(xg[:, :, :].rearrange("p (b d) s -> p b (d s)", b=2), k.ps[:, 6:8, :], ACT.Copy).then_inc(xg_ready, 1)
                    act.wait_ge(combined, b * KT)
                    act.wait_ge(gates_turned, b + 1)
                    nc.scalar.activation(spread[:, :], k.ps[:, 3, :], ACT.Copy).then_inc(spread_ready, 1)

                    def take_ht(ch):
                        n = chunk_tiles(ch) * P
                        act.wait_ge(h_turned, b * CHUNKS + (ch + 1))
                        if ch >= 2:
                            act.wait_ge(down_done, b * CHUNKS + (ch - 1))
                        nc.scalar.activation(ht[:, ch % 2, 0:n], k.ps[:, 2 + ch % 2, 0:n], ACT.Copy).then_inc(ht_ready, 1)

                    for ch in range(CHUNKS + 1):
                        if ch < CHUNKS:
                            n = chunk_tiles(ch) * P
                            act.wait_ge(up_done, b * CHUNKS + (ch + 1))
                            act.wait_ge(h_ready, b * CHUNKS + max(ch - 1, 0))
                            nc.scalar.activation(act_out[:, ch % 2, 0:n], k.ps[:, ch % 2, 0:n], ACT.Silu).then_inc(silu_ready, 1)
                        if ch >= 1:
                            take_ht(ch - 1)
                    act.wait_ge(down_done, b * CHUNKS + CHUNKS)
                    nc.scalar.activation(yb[:, :].rearrange("p (b n) -> p b n", b=2), k.ps[:, 4:6, :], ACT.Copy).then_inc(yb_ready, 1)

        @block.vector
        def _(dve):
            slots = k.con("numbers")

            def place(b):
                for t in range(TT):
                    last = nc.vector.tensor_scalar(hot[:, t, :], slots, r.slot[:, 0, t:t + 1], None, ALU.is_equal)
                last.then_inc(hot1, 1)
                for t in range(TT):
                    nc.vector.tensor_scalar(gated[:, t, :], slots, r.slot[:, 0, t:t + 1], r.gate[:, 0, t:t + 1], ALU.is_equal, ALU.mult)
                    last = nc.vector.tensor_scalar(second[:, t, :], slots, r.slot[:, 1, t:t + 1], r.gate[:, 1, t:t + 1], ALU.is_equal,
                                                   ALU.mult)
                last.then_inc(gated1, 1)
                dve.wait_ge(hot1, b + 1)
                for t in range(TT):
                    last = nc.vector.scalar_tensor_tensor(hot[:, t, :], slots, r.slot[:, 1, t:t + 1], hot[:, t, :], ALU.is_equal, ALU.add)
                last.then_inc(hot_ready, 1)
                dve.wait_ge(gated1, b + 1)
                nc.vector.tensor_tensor(gated[:, :, :], gated[:, :, :], second[:, :, :], ALU.add).then_inc(gated_ready, 1)
                dve.wait_ge(gated_ready, b + 1)
                dve.wait_ge(hot_ready, b + 1)
                nc.vector.tensor_scalar(r.slot[:, :, :], r.slot[:, :, :], -float(SLOTS), None, ALU.add).then_inc(moved, 1)
                dve.wait_ge(moved, b + 1)

            nc.vector.memset(y[:, :, :], 0.0).then_inc(zeroed, 1)
            dve.wait_ge(zeroed, 1)
            place(0)
            used = blocks_used(dve)
            with dve.Fori(0, BLOCKS) as b:
                with dve.If(b < used):
                    for ch in range(CHUNKS):
                        n = chunk_tiles(ch) * P
                        dve.wait_ge(silu_ready, b * CHUNKS + (ch + 1))
                        if ch >= 2:
                            dve.wait_ge(h_turned, b * CHUNKS + (ch - 1))
                        nc.vector.tensor_tensor(hidden[:, ch % 2, 0:n], act_out[:, ch % 2, 0:n], k.ps[:, ch % 2, n:2 * n],
                                                ALU.mult).then_inc(h_ready, 1)
                        if ch == 2:
                            dve.wait_ge(gathered, b + 1)
                            dve.wait_ge(gates_turned, b + 1)
                            place(b + 1)
                    for dt in range(KT):
                        dve.wait_ge(combined, b * KT + (dt + 1))
                        dve.wait_ge(summed, b * KT)
                        nc.vector.tensor_tensor(y[:, dt, :], y[:, dt, :], k.ps[:, 6 + dt % 2, :], ALU.add).then_inc(summed, 1)
            dve.wait_ge(summed, used * KT)
            nc.vector.memset(r.used[:, :], 0).then_inc(finished, 1)
            dve.wait_ge(finished, 1)



def paired_tiles(w1, w3):
    return np.ascontiguousarray(np.stack([tiles(w1), tiles(w3)], axis=2))


def bank_tiles(w):
    return np.ascontiguousarray(w.reshape(w.shape[0] // P, P, -1, BANK).transpose(2, 1, 0, 3))


def up_chunks(w1, w3, first, n, width):
    part = lambda w: w[:, first * P:(first + n * width) * P].reshape(KT, P, n, width * P).transpose(2, 1, 0, 3)
    return np.concatenate([part(w1), part(w3)], axis=3).reshape(n, P, KT * 2 * width * P)


def down_chunks(w2, first, n, width):
    rows_ = w2[first * P:(first + n * width) * P].reshape(n, width, P, D)
    return np.ascontiguousarray(rows_.transpose(0, 2, 1, 3)).reshape(n, P, width * D)


def delta_tiles(w):
    q, kk, v, z = w[:, 0:D], w[:, D:2 * D], w[:, 2 * D:4 * D], w[:, 4 * D:6 * D]
    h = lambda a, i: a[:, i * P:(i + 1) * P]
    out = []
    for g in range(DN_GROUPS):
        out += [h(q, g), h(kk, g), h(v, 2 * g), h(v, 2 * g + 1), h(z, 2 * g), h(z, 2 * g + 1)]
    return tiles(np.concatenate(out, axis=1))


def delta_taps(conv):
    c = conv.reshape(DN_K, 4 * D // P, P)
    order = []
    for g in range(DN_GROUPS):
        order += [g, DN_GROUPS + g, 2 * DN_GROUPS + 2 * g, 2 * DN_GROUPS + 2 * g + 1]
    return c[:, order, :].transpose(2, 1, 0).reshape(P, -1)


def rope_tables(d):
    half = d // 2
    quarter = half // 2
    t = np.arange(LAT)
    inv = np.float32(10000.0) ** (-np.arange(0, half, 2, dtype=np.float32) / np.float32(half))
    cos, sin, swap = np.zeros((P, LAT)), np.zeros((P, LAT)), np.zeros((P, P))
    for p in range(P):
        f = p % d
        position = (t // 64 if f < half else t % 64).astype(np.float32)
        angle = position * inv[f % quarter]
        first = f % half < quarter
        cos[p], sin[p] = np.cos(angle), (-1 if first else 1) * np.sin(angle)
        swap[p + quarter if first else p - quarter, p] = 1
    return np.concatenate([cos, sin, swap], axis=1).astype(np.float32)


def constants():
    s = Smalls()
    i, j = np.arange(P)[:, None], np.arange(P)[None, :]
    s.put("ident", i == j)
    s.put("ones", np.ones((P, P)))
    s.put("tri0", i <= j)
    s.put("tri1", i >= j)
    s.put("keep", np.concatenate([i <= j, i < j, i >= j, i > j], axis=1))
    s.put("beside", np.concatenate([(i >> (b + 1) == j >> (b + 1)) & (i >> b != j >> b) for b in range(LEVELS)], axis=1))
    column = np.arange(2 * (HW + 1))[None, :]
    s.put("halves", (i[:, :1] >= HW) == (column >= HW + 1))
    s.put("ln_rest", np.full((P, 1), np.log(1 - LAM_INIT)))
    s.put("numbers", on_all(np.arange(P)))
    s.put("experts", on_all(np.arange(EXPERTS)))
    s.put("eps", np.full((P, 1), EPS))
    return s


def vectors(a):
    s = Smalls()
    s.put("conds", np.stack([columns(a[n].reshape(-1)) for n in ("c", "c_ctx", "c_2", "c_ctx_2")], axis=2))
    s.put("mod_b", np.concatenate([columns(a["ada_b"][0]), columns(a["ada_b"][1]), columns(a["l0_mod_b_2"]),
                                   columns(a["l1_mod_b_2"])], axis=1))
    s.put("norm_g0", columns(a["norm_g"][0]))
    s.put("norm_g1", columns(a["norm_g"][1]))
    s.put("dn_dt", on_all(a["dn_dt_bias"]))
    s.put("dn_a_log", on_all(a["dn_a_log"]))
    s.put("dn_conv", delta_taps(a["dn_conv_w"][0]))
    m = a["l0_mlstm_conv_w_2"].reshape(3, KT, P)
    s.put("m_conv", m.transpose(2, 1, 0))
    s.put("m_gate_b", on_all(a["l0_mlstm_gate_b_2"]))
    s.put("m_norm_g", columns(a["l0_mlstm_norm_g_2"]))
    s.put("diff_norm_g", columns(a["l0_diff_norm_g_2"]))
    s.put("lambdas", on_all(np.concatenate([a["l0_lambda_q1_2"], a["l0_lambda_q2_2"], a["l0_lambda_k1_2"], a["l0_lambda_k2_2"]])))
    for n in ("l0_mix_pre_g", "l0_mix_post_g", "l0_ffn_pre_g", "l0_ffn_post_g", "l1_mix_pre_g", "l1_mix_post_g", "l1_ffn_pre_g",
              "l1_ffn_post_g", "l1_conv_pw1_b", "l1_conv_dw_b", "l1_conv_ln_g", "l1_conv_ln_b", "l1_conv_pw2_b"):
        s.put(n, columns(a[n + "_2"]))
    s.put("dw_taps", a["l1_conv_dw_w_2"].reshape(CONV_W, KT, P).transpose(2, 1, 0))
    s.put("att_q_g", columns(a["att_q_norm_g"]))
    s.put("att_k_g", columns(a["att_k_norm_g"]))
    s.put("final_g", columns(a["final_norm_g"]))
    s.put("dn_o_g", columns(a["dn_o_norm_g"]))
    return s


def layout(a):
    small, const = vectors(a), constants()
    dn_w = a["dn_w_in"][0]
    arrays = {
        "smalls": small.packed(),
        "consts": const.packed(),
        "tokens": np.ascontiguousarray(np.concatenate([a["ctx"][0], a["x"][0]], axis=0).T.reshape(KT, P, TOK).transpose(1, 0, 2)),
        "mod_w": np.concatenate([bank_tiles(w) for w in (a["ada_w"][0], a["ada_w"][1], a["l0_mod_w_2"], a["l1_mod_w_2"])]),
        "rope": rope_tables(P),
        "rope_2": rope_tables(P // 2),
        "dn_w_ab": rows(dn_w[:, 6 * D:]),
        "dn_w": delta_tiles(dn_w),
        "dn_w_out": tiles(a["dn_w_out"][0]),
        "att_w_kv": tiles(a["att_w_in"][0][:, D:D + 512]),
        "att_w_qz": tiles(np.concatenate([a["att_w_in"][0][:, :D], a["att_w_in"][0][:, D + 512:]], axis=1)),
        "att_w_out": tiles(a["att_w_out"][0]),
    }
    w_in = a["l0_w_in_2"]
    for n, at in (("mq", 0), ("mk", 512), ("mv", 1024), ("mo", 1536), ("dq", 2080), ("dk", 2592), ("dv", 3104)):
        arrays["l0_w_" + n] = tiles(w_in[:, at:at + 512])
    arrays["l0_w_mg"] = rows(w_in[:, 2048:2080])
    arrays["l0_w_out"] = tiles(a["l0_w_out_2"])
    arrays["ctx_2"] = np.ascontiguousarray(a["ctx_2"][0].T.reshape(KT, P, CTX).transpose(1, 0, 2))
    arrays["ffn_up"] = paired_tiles(a["l0_ffn_w1_2"], a["l0_ffn_w3_2"])
    arrays["ffn_down"] = tiles(a["l0_ffn_w2_2"])
    arrays["pw1"] = paired_tiles(a["l1_conv_pw1_w_2"][:, D:], a["l1_conv_pw1_w_2"][:, :D])
    arrays["pw2"] = tiles(a["l1_conv_pw2_w_2"])
    arrays["router"] = rows(a["l1_router_w_2"])
    w1, w3, w2 = a["l1_moe_w1_2"], a["l1_moe_w3_2"], a["l1_moe_w2_2"]
    arrays["moe_up"] = np.concatenate([up_chunks(w1[e], w3[e], 0, WIDE, 2) for e in range(EXPERTS)])
    arrays["moe_up_narrow"] = np.concatenate([up_chunks(w1[e], w3[e], 2 * WIDE, CHUNKS - WIDE, 1) for e in range(EXPERTS)])
    arrays["moe_down"] = np.concatenate([down_chunks(w2[e], 0, WIDE, 2) for e in range(EXPERTS)])
    arrays["moe_down_narrow"] = np.concatenate([down_chunks(w2[e], 2 * WIDE, CHUNKS - WIDE, 1) for e in range(EXPERTS)])
    return arrays, small, const


class Kernel:

    def __init__(self, nc, io):
        self.nc, self.io = nc, io


def program(nc, io, small, const):
    k = Kernel(nc, io)
    with ExitStack() as c:
        sb = lambda n, s: c.enter_context(nc.sbuf_tensor(n, s, FP32))
        k.small = sb("small", [P, small.width])
        k.const = sb("const", [P, const.width])
        k.mod = sb("mod", [P, MOD_TILES, CONDS])
        k.ps = c.enter_context(nc.psum_tensor("ps", [P, 8, BANK], FP32))
        part = lambda t, s: lambda n: t[:, s.at[n][0]:s.at[n][0] + s.at[n][1]]
        k.vec, k.con = part(k.small, small), part(k.const, const)
        k.ident, k.ones, k.eps = k.con("ident"), k.con("ones"), k.con("eps")
        k.tri = (k.con("tri0"), k.con("tri1"))
        k.keep = k.con("keep").rearrange("p (d n) -> p d n", d=2)
        k.beside = [k.con("beside")[:, b * P:(b + 1) * P] for b in range(LEVELS)]

        def modulation(first, cond):
            return k.mod[:, first:first + KT, cond]

        lat = [(CTX, LAT)]
        arena = sb("arena", [P, 2 * KT, TOK])
        x, k.u = arena[:, KT:2 * KT, 0:LAT], arena[:, 0:KT, :]
        with ExitStack() as c0:
            og = arena
            with ExitStack() as c1:
                u = c1.enter_context(nc.sbuf_tensor("u0", [P, KT, TOK], FP32))
                k.dn_gate = c1.enter_context(nc.sbuf_tensor("dn_gate", [P, DN_GROUPS, 4, 2, NC6, 2], FP32))
                with nc.sbuf_tensor("h0", [P, KT, TOK], FP32) as h0:
                    load_once(k, h0)
                    modulations(k)
                    norm_modulate(k, "n0", h0, u, TOK, k.vec("norm_g0"),
                                  [(0, CTX, modulation(8, 1), modulation(0, 1)), (CTX, LAT, modulation(8, 0), modulation(0, 0))])
                delta_gates(k, u)
                delta_rule(k, u, og)
            recycle(k)
            with ExitStack() as c1:
                h = c1.enter_context(nc.sbuf_tensor("h", [P, KT, TOK], FP32))
                load(k, "tokens_again", h[:, :, :], "tokens")
                linear(k, "dn_out", k.io["dn_w_out"], lambda kt, t0, n: og[:, kt, t0:t0 + n], 2 * KT, KT, spans_of(TOK),
                       add_tile(k, h, [(16, 1), (16, 0)]))
                with ExitStack() as c2:
                    sb2 = lambda n, s: c2.enter_context(nc.sbuf_tensor(n, s, FP32))
                    u = sb2("u1", [P, KT, TOK])
                    norm_modulate(k, "n1", h, u, TOK, k.vec("norm_g1"),
                                  [(0, CTX, modulation(32, 1), modulation(24, 1)), (CTX, LAT, modulation(32, 0), modulation(24, 0))])
                    kv, q, z = sb2("att_kv", [P, 4, TOK]), sb2("att_q", [P, KT, LAT]), og[:, 0:KT, 0:LAT]
                    linear(k, "att_kv", k.io["att_w_kv"], lambda kt, t0, n: u[:, kt, t0:t0 + n], KT, 4, spans_of(TOK),
                           take_tile(k, "vector", kv))
                    linear(k, "att_q", k.io["att_w_qz"][0:KT], lambda kt, t0, n: u[:, kt, t0:t0 + n], KT, KT, lat,
                           take_tile(k, "vector", q), unroll=4)
                    linear(k, "att_z", k.io["att_w_qz"][KT:2 * KT], lambda kt, t0, n: u[:, kt, t0:t0 + n], KT, KT, lat,
                           take_tile(k, "scalar", z, ACT.Silu), unroll=4, on="scalar")
                    tables = sb2("rope_sb", [P, 2 * LAT + P])
                    load(k, "rope_tables", tables[:, :], "rope")
                    rope = (tables[:, 2 * LAT:2 * LAT + P], tables[:, 0:LAT], tables[:, LAT:2 * LAT])
                    rotary(k, "rk", kv, 2, TOK, k.vec("att_k_g"), *rope)
                    rotary(k, "rq", q, KT, LAT, k.vec("att_q_g"), *rope)
                    vtok = sb2("att_vtok", [P, 2, NC6, P])
                    token_major(k, "att_v", lambda t, ch: kv[:, 2 + t, ch * P:(ch + 1) * P], 2, vtok)
                    mixed = u[:, :, 0:LAT]
                    attend(k, "att", q, kv, vtok, mixed, 2, 4, True, 1, float(P) ** -0.5, z=z)
                    linear(k, "att_out", k.io["att_w_out"], lambda kt, t0, n: mixed[:, kt, :], KT, KT, [(0, LAT)],
                           add_tile(k, h[:, :, CTX:TOK], [(40, 0)]), unroll=4)
                recycle(k)
                take_x(k, h, x, k.vec("final_g"))
        recycle(k)
        second_block(k, x)
        store(k, "out", x[:, :, :])


_OUTS = [((P, KT, LAT), "float32")]


def kernel(**inputs):
    import concourse.bacc as bacc
    from concourse.bass_utils import run_bass_kernel_spmd

    inputs = {n: np.asarray(v) for n, v in inputs.items()}
    arrays, small, const = layout(inputs)
    nc = bacc.Bacc("TRN2", target_bir_lowering=False, num_devices=1)
    io = {n: nc.dram_tensor(n, a.shape, mybir.dt.from_np(a.dtype), kind="ExternalInput").ap() for n, a in arrays.items()}
    io["out"] = nc.dram_tensor("out", (P, KT, LAT), FP32, kind="ExternalOutput").ap()
    program(nc, io, small, const)
    result = run_bass_kernel_spmd(nc, [arrays], core_ids=[0]).results[0]["out"]
    return np.ascontiguousarray(result.transpose(2, 1, 0)).reshape(1, LAT, D)
```
